# Optimizing a Trainium2 kernel written in Bass

```python
import math
import jax, jax.numpy as jnp
from jax import lax
import numpy as np

D_MODEL = 1024
BATCH = 1
SEQ = 512
DEPTH = 2

N_MIXERS = 2
N_CONV = (DEPTH + 1) // 2
N_ATTN = DEPTH // 2
CONV_WIDTH = 31
N_HEADS = 16
HEAD_DIM = D_MODEL // N_HEADS
BLOCK_Q = 128
PEER_HEADS = 8
PEER_DQ = 256
PEER_DQH = PEER_DQ // 2
N_KEYS = 128
N_EXPERTS = N_KEYS * N_KEYS
PEER_TOPK = 16
PEER_CHUNK = 128
ADA_CHUNKS = 6
EPS = 1e-6

kernel_name = 'hybrid_conv_stickbreak_peer_adaln'

def _rmsnorm(x, g):
    x32 = x.astype(jnp.float32)
    y = x32 * lax.rsqrt(jnp.mean(x32 * x32, axis=-1, keepdims=True) + EPS)
    return y.astype(x.dtype) * g

def _layernorm(x, g, b):
    x32 = x.astype(jnp.float32)
    mu = jnp.mean(x32, axis=-1, keepdims=True)
    var = jnp.mean(jnp.square(x32 - mu), axis=-1, keepdims=True)
    y = (x32 - mu) * lax.rsqrt(var + EPS)
    return y.astype(x.dtype) * g + b

def _conformer_conv(h, w_in, b_in, w_dw, b_dw, ln_g, ln_b, w_out, b_out):
    a, gate = jnp.split(h @ w_in + b_in, 2, axis=-1)
    u = a * jax.nn.sigmoid(gate)
    u = lax.conv_general_dilated(
        u, w_dw[:, None, :], window_strides=(1,),
        padding=[(CONV_WIDTH - 1, 0)],
        dimension_numbers=('NWC', 'WIO', 'NWC'),
        feature_group_count=D_MODEL) + b_dw
    u = jax.nn.silu(_layernorm(u, ln_g, ln_b))
    return u @ w_out + b_out

def _stick_breaking_attention(h, w_qkv, w_o):
    B, S, _ = h.shape
    qkv = (h @ w_qkv).reshape(B, S, 3, N_HEADS, HEAD_DIM)
    q = jnp.transpose(qkv[:, :, 0], (0, 2, 1, 3))
    k = jnp.transpose(qkv[:, :, 1], (0, 2, 1, 3))
    v = jnp.transpose(qkv[:, :, 2], (0, 2, 1, 3))
    scale = 1.0 / math.sqrt(HEAD_DIM)
    outs = []
    for blk in range(S // BLOCK_Q):
        q0 = blk * BLOCK_Q
        kend = q0 + BLOCK_Q
        qb = q[:, :, q0:kend]
        kb = k[:, :, :kend]
        vb = v[:, :, :kend]
        z = jnp.einsum('bhqd,bhkd->bhqk', qb, kb).astype(jnp.float32) * scale
        t_idx = q0 + jnp.arange(BLOCK_Q)[:, None]
        s_idx = jnp.arange(kend)[None, :]
        mask = s_idx < t_idx
        log_beta = jax.nn.log_sigmoid(z)
        log_1m = jnp.where(mask, -jax.nn.softplus(z), 0.0)
        log_w = log_beta + lax.cumsum(log_1m, axis=3, reverse=True) - log_1m
        a = jnp.where(mask, jnp.exp(log_w), 0.0).astype(vb.dtype)
        outs.append(jnp.einsum('bhqk,bhkd->bhqd', a, vb))
    o = jnp.concatenate(outs, axis=2)
    o = jnp.transpose(o, (0, 2, 1, 3)).reshape(B, S, N_HEADS * HEAD_DIM)
    return o @ w_o

def _peer(h, w_q, sub_keys, u_tab, v_tab):
    B, S, D = h.shape
    T = B * S
    hf = h.reshape(T, D)
    q = (hf @ w_q).reshape(T, PEER_HEADS, 2, PEER_DQH)
    s = jnp.einsum('thcd,hcnd->thcn', q, sub_keys).astype(jnp.float32)
    top_s, top_i = lax.top_k(s, PEER_TOPK)
    cand = (top_s[:, :, 0, :, None] + top_s[:, :, 1, None, :]).reshape(
        T, PEER_HEADS, PEER_TOPK * PEER_TOPK)
    best_s, best_c = lax.top_k(cand, PEER_TOPK)
    i1 = jnp.take_along_axis(top_i[:, :, 0], best_c // PEER_TOPK, axis=-1)
    i2 = jnp.take_along_axis(top_i[:, :, 1], best_c % PEER_TOPK, axis=-1)
    experts = i1 * N_KEYS + i2
    gates = jax.nn.softmax(best_s, axis=-1).astype(h.dtype)
    n_chunk = T // PEER_CHUNK
    hk = PEER_HEADS * PEER_TOPK
    xs = hf.reshape(n_chunk, PEER_CHUNK, D)
    es = experts.reshape(n_chunk, PEER_CHUNK, hk)
    gs = gates.reshape(n_chunk, PEER_CHUNK, hk)

    def chunk(args):
        xc, ec, gc = args
        u_sel = u_tab[ec]
        act = jax.nn.gelu(jnp.einsum('tkd,td->tk', u_sel, xc), approximate=False) * gc
        return jnp.einsum('tk,tkd->td', act, v_tab[ec])

    y = lax.map(chunk, (xs, es, gs))
    return y.reshape(B, S, D)

def setup_inputs(seed: int = 0) -> dict:
    key = jax.random.key(seed)
    ks = jax.random.split(key, 24)
    D = D_MODEL
    n = jax.random.normal
    f = jnp.float32
    inv = D ** -0.5
    return {
        'x': n(ks[0], (BATCH, SEQ, D), f),
        'c': n(ks[1], (BATCH, D), f),
        'ada_w': n(ks[2], (DEPTH, D, ADA_CHUNKS * D), f) * (0.5 * inv),
        'ada_b': n(ks[3], (DEPTH, ADA_CHUNKS * D), f) * 0.01,
        'norm_mix_g': 1.0 + 0.02 * n(ks[4], (DEPTH, D), f),
        'norm_ffn_g': 1.0 + 0.02 * n(ks[5], (DEPTH, D), f),
        'cv_w_in': n(ks[6], (N_CONV, D, 2 * D), f) * inv,
        'cv_b_in': n(ks[7], (N_CONV, 2 * D), f) * 0.01,
        'cv_w_dw': n(ks[8], (N_CONV, CONV_WIDTH, D), f) * CONV_WIDTH ** -0.5,
        'cv_b_dw': n(ks[9], (N_CONV, D), f) * 0.01,
        'cv_ln_g': 1.0 + 0.02 * n(ks[10], (N_CONV, D), f),
        'cv_ln_b': n(ks[11], (N_CONV, D), f) * 0.01,
        'cv_w_out': n(ks[12], (N_CONV, D, D), f) * inv,
        'cv_b_out': n(ks[13], (N_CONV, D), f) * 0.01,
        'sb_w_qkv': n(ks[14], (N_ATTN, D, 3 * N_HEADS * HEAD_DIM), f) * inv,
        'sb_w_o': n(ks[15], (N_ATTN, N_HEADS * HEAD_DIM, D), f) * (N_HEADS * HEAD_DIM) ** -0.5,
        'pk_w_q': n(ks[16], (DEPTH, D, PEER_HEADS * PEER_DQ), f) * inv,
        'pk_keys': n(ks[17], (DEPTH, PEER_HEADS, 2, N_KEYS, PEER_DQH), f) * PEER_DQH ** -0.5,
        'pk_u': n(ks[18], (DEPTH, N_EXPERTS, D), f) * inv,
        'pk_v': n(ks[19], (DEPTH, N_EXPERTS, D), f),
        'final_g': 1.0 + 0.02 * n(ks[20], (D,), f),
    }

def reference(x, c, ada_w, ada_b, norm_mix_g, norm_ffn_g, cv_w_in, cv_b_in, cv_w_dw,
              cv_b_dw, cv_ln_g, cv_ln_b, cv_w_out, cv_b_out, sb_w_qkv, sb_w_o,
              pk_w_q, pk_keys, pk_u, pk_v, final_g):
    c_act = jax.nn.silu(c)
    for i in range(DEPTH):
        mod = (c_act @ ada_w[i] + ada_b[i])[:, None, :]
        sh1, sc1, g1, sh2, sc2, g2 = jnp.split(mod, ADA_CHUNKS, axis=-1)
        h = _rmsnorm(x, norm_mix_g[i]) * (1.0 + sc1) + sh1
        j = i // N_MIXERS
        if i % N_MIXERS == 0:
            m = _conformer_conv(h, cv_w_in[j], cv_b_in[j], cv_w_dw[j], cv_b_dw[j],
                                cv_ln_g[j], cv_ln_b[j], cv_w_out[j], cv_b_out[j])
        else:
            m = _stick_breaking_attention(h, sb_w_qkv[j], sb_w_o[j])
        x = x + g1 * m
        h = _rmsnorm(x, norm_ffn_g[i]) * (1.0 + sc2) + sh2
        x = x + g2 * _peer(h, pk_w_q[i], pk_keys[i], pk_u[i], pk_v[i])
    return _rmsnorm(x, final_g)


_drawn_inputs = setup_inputs


def setup_inputs(seed=0):
    import zlib

    import numpy as np

    out = dict(_drawn_inputs(seed))
    spreads = {}
    factors = {'norm_mix_g': 2.736,
     'cv_b_in': 4.221,
     'cv_b_dw': 3.205,
     'cv_ln_g': 2.922,
     'cv_ln_b': 4.126,
     'cv_b_out': 3.014,
     'final_g': 2.939}
    for name, (base, spread) in spreads.items():
        noise = np.random.default_rng([zlib.crc32(name.encode()), seed]).standard_normal(out[name].shape)
        drawn = base * np.exp(spread * noise) if base else spread * noise
        out[name] = __import__('jax').numpy.asarray(drawn.astype(out[name].dtype))
    for name, factor in factors.items():
        out[name] = (out[name] * factor).astype(out[name].dtype)
    return out
```

```python
from contextlib import ExitStack, contextmanager

import concourse.bass as bass
from concourse import mybir

F32 = mybir.dt.float32
I32 = mybir.dt.int32
U32 = mybir.dt.uint32
ALU = mybir.AluOpType
ACT = mybir.ActivationFunctionType
AX = mybir.AxisListType

P = 128
D = 1024
SEQ = 512
DEPTH = 2
KB = D // P
TILES = SEQ // P
HALF = 2 * P
WIDTH = 31
HEADS = 16
HD = D // HEADS
PAIRS = HEADS // 2
PH = 8
NK = 128
TOPK = 16
PICKS = PH * TOPK
EPS = 1e-6
LOWEST = -3.0e38

NC = 256
CHUNK = KB * NC
SLOT = CHUNK + 2 * NK
UR = 8
VR = 4
BATCH = 8
BATCHES = PICKS // BATCH
JOBS = DEPTH * TILES

COLS = {}
_at = 0
for _name, _n in (("c", KB), ("g_mix", DEPTH * KB), ("g_ffn", DEPTH * KB), ("b_in", 2 * KB), ("w_dw", KB * WIDTH),
                  ("b_dw", KB), ("ln_g", KB), ("ln_b", KB)):
    COLS[_name] = (_at, _n)
    _at += _n
N_COLS = _at

CHAIN = [("ada", 0, 0, 24),
         ("glu", 0, 0, 8), ("out", 0, 0, 4), ("pk", 0, 0, 8),
         ("glu", 0, 1, 8), ("out", 0, 1, 4), ("pk", 0, 1, 8),
         ("ada", 1, 0, 24),
         ("qkv", 1, 0, 12), ("out", 1, 0, 4), ("pk", 1, 0, 8),
         ("qkv", 1, 1, 12), ("out", 1, 1, 4), ("pk", 1, 1, 8)]
BASE = {}
_n = 0
for _s, _l, _h, _k in CHAIN:
    BASE[_s, _l, _h] = _n
    _n += _k
ADA_CHUNKS = 24
ADA_KEPT = 20


class Steps:

    def __init__(self, engine, sem, met):
        self.engine, self.sem, self.met, self.count, self.static = engine, sem, met, 0, 0

    def apart(self):
        self.engine.sem_inc(self.met, 1)

    def __call__(self, instruction):
        instruction.then_inc(self.sem, 1)
        self.count = self.count + 1
        self.static += 1
        self.engine.wait_ge(self.sem, self.count)

    @contextmanager
    def loop(self, times, per):
        base, static = self.count, self.static
        with self.engine.Fori(0, times) as i:
            self.count = i * per + base
            yield i
            assert self.static - static == per, (self.static - static, per)
        self.count, self.static = base + times * per, static + times * per


def build(nc, a, out):
    with ExitStack() as ctx:
        def sb(name, shape, dt=F32):
            return ctx.enter_context(nc.sbuf_tensor(name, shape, dt))

        def ps(name):
            return ctx.enter_context(nc.psum_tensor(name, [P, 512], F32))

        def sem(name):
            return ctx.enter_context(nc.semaphore(name))

        x = sb("x", [P, TILES, D])
        mod_rows = sb("mod_rows", [P, 3 * D])
        g1_row, sh2_row, sc2_row = (mod_rows[:, i * D:(i + 1) * D] for i in range(3))
        g2_row = sb("g2_row", [P, DEPTH, D])
        u_rows = sb("u_rows", [P, UR, D])
        v_rows = sb("v_rows", [P, VR, D])
        diag = sb("diag", [P, BATCH, P])
        weights = sb("weights", [P, 2, SLOT])
        h_rows = sb("h_rows", [P, 3, D])
        xn = sb("xn", [P, D])
        y_tmp = sb("y_tmp", [P, 512])
        region = sb("region", [P, 14336])
        qs = sb("qs", [P, 2, 512])
        cols = sb("cols", [P, N_COLS])
        mod_cols = sb("mod_cols", [P, 4, KB])
        c_act = sb("c_act", [P, KB])
        bias_row = sb("bias_row", [1, 2, NC])
        ident = sb("ident", [P, P])
        ones_mean = sb("ones_mean", [P, P])
        one_row = sb("one_row", [1, P])
        zero_row = sb("zero_row", [1, P])
        zero_wide = sb("zero_wide", [1, 512])
        keep_past = sb("keep_past", [P, P])
        not_past = sb("not_past", [P, P])
        iota16 = sb("iota16", [P, TOPK])
        eps_col = sb("eps_col", [P, 1])
        sumsq = sb("sumsq", [P, 1])
        root = sb("root", [P, 1])
        rstd = sb("rstd", [P, 1])
        pick_idx = sb("pick_idx", [P, 4, PICKS], I32)
        pick_gate = sb("pick_gate", [P, 4, PICKS])
        idx_now = sb("idx_now", [P, 2, 2, BATCH], I32)
        dots = sb("dots", [P, 2, PICKS])
        acts = sb("acts", [P, 2, PICKS])
        list_ = sb("list_", [P, 2, NK])
        rest = sb("rest", [P, 2 * NK])
        top = sb("top", [P, 2, TOPK])
        top_i = sb("top_i", [P, 2, TOPK], U32)
        top_f = sb("top_f", [P, 2, TOPK])
        cand = sb("cand", [P, TOPK * TOPK])
        best = sb("best", [P, TOPK])
        best_i = sb("best_i", [P, TOPK], U32)
        place_i = sb("place_i", [P, 2, TOPK], U32)
        place_f = sb("place_f", [P, 2, TOPK])
        onehot = sb("onehot", [P, 2, TOPK, TOPK])
        best_of = sb("best_of", [P, 2, TOPK])
        pre_idx = sb("pre_idx", [P, TOPK])
        best_all = sb("best_all", [P, PH, TOPK])
        gate_sum = sb("gate_sum", [P, PH])
        gate_inv = sb("gate_inv", [P, PH])

        keys_t = region[:, 0:4096].rearrange("p (k t) -> p k t", k=KB)
        values = region[:, 4096:8192].rearrange("p (t n) -> p t n", t=TILES)
        q_t = region[:, 8192:10240].rearrange("p (k t) -> p k t", k=KB)
        beta = region[:, 10240:11264].rearrange("p (t n) -> p t n", t=2)
        stay = region[:, 11264:12288].rearrange("p (t n) -> p t n", t=2)
        a_t = region[:, 12288:14336].rearrange("p (e j q) -> p e j q", e=2, q=HALF)
        h_t = region[:, 12288:14336].rearrange("p (k t) -> p k t", k=KB)
        scores = region[:, 8192:12288].rearrange("p (t n) -> p t n", t=2)
        PAST = WIDTH - 1
        u_t = region[:, 0:KB * (PAST + HALF)].rearrange("p (k t) -> p k t", k=KB)
        c_t = region[:, 2288:4336].rearrange("p (k t) -> p k t", k=KB)
        c_sq = region[:, 4336:6384].rearrange("p (k t) -> p k t", k=KB)
        gate_sig = region[:, 6384:6896].rearrange("p (s t) -> p s t", s=2)
        ln_rstd = region[:, 6896:7152]
        b_out_row = region[:, 7168:8192]
        sh1_row = region[:, 0:1024]
        sc1_row = region[:, 1024:2048]
        g_ffn_row = region[:, 2048:3072]
        c_wide = region[:, 3072:4096].rearrange("p (k m) -> p k m", k=KB)
        final_row = region[:, 0:1024]

        acc_v = [ps("acc_v0"), ps("acc_v1")]
        acc = [ps("acc0"), ps("acc1")]
        mid = [ps("mid0"), ps("mid1")]
        zed = [ps("zed0"), ps("zed1")]

        def col(name, i=None, n=1):
            at, size = COLS[name]
            return cols[:, at:at + size] if i is None else cols[:, bass.ds(i + at, n)]

        cols_in, x_in, b_out_in, g_ffn_in, final_in = map(sem, ("cols_in", "x_in", "b_out_in", "g_ffn_in", "final_in"))
        consts_ready = sem("consts_ready")
        weights_in = [sem(f"weights_in{i}") for i in range(2)]
        bias_in = [sem(f"bias_in{i}") for i in range(2)]
        acc_full, acc_free = sem("acc_full"), sem("acc_free")
        c_silu_ready, c_wide_ready, cols_full, mod_ready = map(sem, ("c_silu_ready", "c_wide_ready", "cols_full", "mod_ready"))
        root_ready, rstd_ready, xn_ready, xn_t_full, h_t_ready, h_rows_ready = map(
            sem, ("root_ready", "rstd_ready", "xn_ready", "xn_t_full", "h_t_ready", "h_rows_ready"))
        sig_ready, conv_ready, mean_full, centred, squared, var_full, dev_ready, normed, silu_ready = map(
            sem, ("sig_ready", "conv_ready", "mean_full", "centred", "squared", "var_full", "dev_ready", "normed", "silu_ready"))
        scores_full, scores_ready = map(sem, ("scores_full", "scores_ready"))
        best_ready, exp_ready, picks_ready = map(sem, ("best_ready", "exp_ready", "picks_ready"))
        z_full, sigs_ready, a_ready, a_t_full, a_t_ready, o_full, o_ready = map(
            sem, ("z_full", "sigs_ready", "a_ready", "a_t_full", "a_t_ready", "o_full", "o_ready"))
        idx_staged = sem("idx_staged")
        u_in = [sem(f"u_in{i}") for i in range(UR)]
        v_in = [sem(f"v_in{i}") for i in range(VR)]
        u_used, v_used = sem("u_used"), sem("v_used")
        dots_ready, gelu_ready, acts_ready, diag_ready, y_full, x_peer = map(
            sem, ("dots_ready", "gelu_ready", "acts_ready", "diag_ready", "y_full", "x_peer"))
        act_steps, dve_steps, pool_steps = sem("act_steps"), sem("dve_steps"), sem("pool_steps")
        pool_waits_met, dve_waits_met = sem("pool_waits_met"), sem("dve_waits_met")
        out_ready, stored = sem("out_ready"), sem("stored")

        CREDIT = 2
        U_CREDIT, V_CREDIT = UR, 2 * VR

        def acc_done(stage, l, h):
            return CREDIT + BASE[stage, l, h] + {s[:3]: s[3] for s in CHAIN}[stage, l, h]

        def half_no(l, h):
            return 2 * l + h

        def norm_no(l, h, which, tt):
            return (half_no(l, h) * 2 + which) * 2 + tt

        N_NORMS = 4 * 2 * DEPTH
        PK = {(l, h): half_no(l, h) * 8 for l in range(DEPTH) for h in range(2)}
        block = ctx.enter_context(nc.Block())

        ORDER = [("ada", 0, 0), ("mix", 0, 0), ("sel", 0, 0), ("seg", 0), ("mix", 0, 1), ("sel", 0, 1), ("ada", 1, 0),
                 ("seg", 1), ("seg", 2), ("seg", 3), ("mix", 1, 0), ("sel", 1, 0), ("seg", 4), ("seg", 5),
                 ("mix", 1, 1), ("sel", 1, 1), ("seg", 6), ("seg", 7), ("seg", 8), ("final",)]

        @block.sync
        def _(sp):
            sp.dma_start(cols[:, :], a["cols"]).then_inc(cols_in, 16)
            src = {("ada", l, 0): a[f"ada{l}"] for l in range(DEPTH)}
            for h in range(2):
                src |= {("glu", 0, h): a["w_in"], ("out", 0, h): a["w_out"], ("qkv", 1, h): a["w_qkv"],
                        ("out", 1, h): a["w_o"], ("pk", 0, h): a["pk0"], ("pk", 1, h): a["pk1"]}
            pk_before = 0
            for at, (stage, l, h, count) in enumerate(CHAIN):
                base = BASE[stage, l, h]
                width = SLOT if stage == "pk" else CHUNK
                source = src[stage, l, h]
                before = CHAIN[at - 1][0] if at else None

                def load(i, s, free, value):
                    if free is not None:
                        sp.wait_ge(free, value)
                    sp.dma_start(weights[:, s, 0:width], source[bass.ds(i, 1), :, :].rearrange("a p n -> p (a n)")
                                 ).then_inc(weights_in[s], 16)
                    if stage == "ada":
                        sp.dma_start(bias_row[0:1, s, :], a["ada_b"][l:l + 1, bass.ds(i * NC, NC)]).then_inc(bias_in[s], 16)

                for s in range(2):
                    if before is None:
                        load(s, s, None, 0)
                    elif before == "pk":
                        load(s, s, scores_full, pk_before - 1 + s)
                    else:
                        load(s, s, acc_full, base - 1 + s)
                if stage == "ada":
                    if l == 0:
                        sp.dma_start(x[:, :, :], a["x"].rearrange("(t p) d -> p t d", p=P)).then_inc(x_in, 16)
                        sp.dma_start(b_out_row, a["b_out"].partition_broadcast(P)).then_inc(b_out_in, 16)
                    else:
                        sp.wait_ge(acc_free, acc_done("out", 0, 1))
                    sp.dma_start(g_ffn_row, a["g_ffn"][l, :].partition_broadcast(P)).then_inc(g_ffn_in, 16)
                with sp.Fori(1, count // 2) as i:
                    for s in range(2):
                        if stage == "pk":
                            load(i * 2 + s, s, scores_full, i * 2 + (PK[l, h] - 1 + s))
                        else:
                            load(i * 2 + s, s, acc_full, i * 2 + (base - 1 + s))
                if stage == "pk":
                    pk_before = PK[l, h] + 8
            sp.wait_ge(o_ready, 2 * HEADS)
            sp.dma_start(final_row, a["final_g"].partition_broadcast(P)).then_inc(final_in, 16)
            for t in range(TILES):
                sp.wait_ge(out_ready, t + 1)
                sp.dma_start(out[t * P:(t + 1) * P, :], x[:, t, :]).then_inc(stored, 16)
            sp.wait_ge(stored, 16 * TILES)

        @block.gpsimd
        def _(pool):
            steps = Steps(pool, pool_steps, pool_waits_met)
            steps(nc.gpsimd.memset(ident[:, :], 0.0))
            steps(nc.gpsimd.affine_select(out=ident[:, :], in_=ident[:, :], compare_op=ALU.not_equal, fill=1.0,
                                          base=0, pattern=[[-1, P]], channel_multiplier=1))
            steps(nc.gpsimd.memset(keep_past[:, :], 1.0))
            steps(nc.gpsimd.affine_select(out=keep_past[:, :], in_=keep_past[:, :], compare_op=ALU.is_gt, fill=0.0,
                                          base=0, pattern=[[-1, P]], channel_multiplier=1))
            steps(nc.gpsimd.memset(not_past[:, :], 0.0))
            steps(nc.gpsimd.affine_select(out=not_past[:, :], in_=not_past[:, :], compare_op=ALU.is_gt, fill=1.0,
                                          base=0, pattern=[[-1, P]], channel_multiplier=1))
            steps(nc.gpsimd.iota(iota16[:, :], pattern=[[1, TOPK]], base=0, channel_multiplier=0,
                                 allow_small_or_imprecise_dtypes=True))
            steps(nc.gpsimd.memset(ones_mean[:, :], 1.0 / D))
            steps(nc.gpsimd.memset(one_row[:, :], 1.0))
            steps(nc.gpsimd.memset(zero_row[:, :], 0.0))
            steps(nc.gpsimd.memset(zero_wide[:, :], 0.0))
            nc.gpsimd.memset(eps_col[:, :], EPS).then_inc(consts_ready, 1)
            pool.sem_inc(u_used, U_CREDIT)

            def gather(us, vs, it):
                for par in range(2):
                    b = it * 2 + par
                    if us is not None:
                        pool.wait_ge(u_used, (b + us * BATCHES) * BATCH + 1)
                        steps(nc.gpsimd.tensor_copy(idx_now[:, 0, par, :], pick_idx[:, us % 4, bass.ds(b * BATCH, BATCH)]))
                    if vs is not None:
                        pool.wait_ge(v_used, (b + vs * BATCHES) * BATCH + 1 + V_CREDIT - VR)
                        steps(nc.gpsimd.tensor_copy(idx_now[:, 1, par, :], pick_idx[:, vs % 4, bass.ds(b * BATCH, BATCH)]))
                    for r in range(BATCH):
                        if us is not None:
                            pool.wait_ge(u_used, (b + us * BATCHES) * BATCH + (r + 1))
                            steps.apart()
                            nc.gpsimd.indirect_dma_start(u_rows[:, r, :], None, a["pk_u"], bass.IndirectOffsetOnAxis(
                                ap=idx_now[:, 0, par, r:r + 1], axis=0)).then_inc(u_in[r], 16)
                        if vs is not None:
                            pool.wait_ge(v_used, (b + vs * BATCHES) * BATCH + (r + 1 + V_CREDIT - VR))
                            steps.apart()
                            nc.gpsimd.indirect_dma_start(v_rows[:, r % VR, :], None, a["pk_v"], bass.IndirectOffsetOnAxis(
                                ap=idx_now[:, 1, par, r:r + 1], axis=0)).then_inc(v_in[r % VR], 16)

            for s in range(JOBS + 1):
                us, vs = (s if s < JOBS else None), (s - 1 if s else None)
                if us is not None:
                    pool.wait_ge(picks_ready, us + 1)
                per = 2 * ((us is not None) + (vs is not None))
                with steps.loop(BATCHES // 2, per) as it:
                    gather(us, vs, it)

        @block.tensor
        def _(pe):
            pe.sem_inc(acc_free, CREDIT)
            pe.sem_inc(scores_ready, CREDIT)
            pe.sem_inc(v_used, V_CREDIT)
            pe.wait_ge(consts_ready, 1)

            def chunks(stage, l, h, product):
                base = BASE[stage, l, h]
                count = {c[:3]: c[3] for c in CHAIN}[stage, l, h]
                with pe.Fori(0, count // 2) as i:
                    for s in range(2):
                        pe.wait_ge(weights_in[s], i * 16 + (base // 2 + 1) * 16)
                        pe.wait_ge(acc_free, i * 2 + (base + s + 1))
                        product(s, i).then_inc(acc_full, 1)

            def by_token(lhs):
                def product(s, i):
                    for tt in range(2):
                        for k in range(KB):
                            last = nc.tensor.matmul(acc[s][:, tt * NC:(tt + 1) * NC], lhs(k, tt),
                                                    weights[:, s, k * NC:(k + 1) * NC], start=k == 0, stop=k == KB - 1)
                    return last
                return product

            def by_channel(s, i):
                for c in range(2):
                    for k in range(KB):
                        last = nc.tensor.matmul(acc[s][:, c * HALF:(c + 1) * HALF],
                                                weights[:, s, k * NC + c * P:k * NC + (c + 1) * P], h_t[:, k, :],
                                                start=k == 0, stop=k == KB - 1)
                return last

            def norm(l, h, which):
                for tt in range(2):
                    n = norm_no(l, h, which, tt)
                    pe.wait_ge(xn_ready, n + 1)
                    if n:
                        pe.wait_ge(h_t_ready, n)
                    for g in range(2):
                        for j in range(4):
                            k = 4 * g + j
                            last = nc.tensor.transpose(mid[g][:, j * P:(j + 1) * P], xn[:, k * P:(k + 1) * P], ident[:, :])
                        last.then_inc(xn_t_full, 1)

            def ada(l):
                pe.wait_ge(c_wide_ready, l + 1)

                def product(s, i):
                    for k in range(KB):
                        nc.tensor.matmul(acc[s][:, 0:NC], c_wide[:, k, :], weights[:, s, k * NC:(k + 1) * NC],
                                         start=k == 0, stop=False)
                    pe.wait_ge(bias_in[s], i * 16 + (l * ADA_CHUNKS // 2 + 1) * 16)
                    return nc.tensor.matmul(acc[s][:, 0:NC], one_row[0:1, :], bias_row[0:1, s, :], start=False, stop=True)
                chunks("ada", l, 0, product)
                pe.wait_ge(acc_free, acc_done("ada", l, 0))
                for m, row in enumerate((sh1_row, sc1_row, sh2_row, sc2_row)):
                    for k in range(KB):
                        at = m * KB + k
                        last = nc.tensor.matmul(mid[0][:, at:at + 1], row[0:1, k * P:(k + 1) * P], one_row[0:1, 0:1],
                                                start=True, stop=True)
                last.then_inc(cols_full, 1)

            def conv(h):
                pe.wait_ge(h_t_ready, norm_no(0, h, 0, 1) + 1)
                chunks("glu", 0, h, by_channel)
                pe.wait_ge(conv_ready, h + 1)
                for k in range(KB):
                    last = nc.tensor.matmul(mid[0][:, 0:HALF], ones_mean[:, :], c_t[:, k, :], start=k == 0, stop=k == KB - 1)
                last.then_inc(mean_full, 1)
                pe.wait_ge(squared, h + 1)
                for k in range(KB):
                    last = nc.tensor.matmul(mid[1][:, 0:HALF], ones_mean[:, :], c_sq[:, k, :], start=k == 0, stop=k == KB - 1)
                last.then_inc(var_full, 1)
                pe.wait_ge(silu_ready, h + 1)
                chunks("out", 0, h, by_token(lambda k, tt: c_t[:, k, tt * P:(tt + 1) * P]))

            def attention(h):
                pe.wait_ge(h_t_ready, norm_no(1, h, 0, 1) + 1)
                with pe.Fori(0, 4) as i:
                    for s in range(2):
                        base = BASE["qkv", 1, h]
                        pe.wait_ge(weights_in[s], i * 16 + (base // 2 + 1) * 16)
                        pe.wait_ge(acc_free, i * 2 + (base + s + 1))
                        by_channel(s, i).then_inc(acc_full, 1)
                with pe.Fori(0, 2) as i:
                    for s in range(2):
                        base = BASE["qkv", 1, h] + 8
                        pe.wait_ge(weights_in[s], i * 16 + (base // 2 + 1) * 16)
                        pe.wait_ge(acc_free, i * 2 + (base + s + 1))
                        by_token(lambda k, tt: h_t[:, k, tt * P:(tt + 1) * P])(s, i).then_inc(acc_full, 1)
                pe.wait_ge(acc_free, acc_done("qkv", 1, h))

                def keys_seen(tt):
                    return (2 * h + tt + 1) * P

                def logits(head, tt):
                    p, e = head // 2, head % 2
                    unit = (h * HEADS + head) * 2 + tt
                    if unit >= 2:
                        pe.wait_ge(sigs_ready, unit - 1)
                    nc.tensor.matmul(zed[tt][:, 0:keys_seen(tt)], q_t[e * HD:(e + 1) * HD, p, tt * P:(tt + 1) * P],
                                     keys_t[e * HD:(e + 1) * HD, p, 0:keys_seen(tt)], start=True, stop=True
                                     ).then_inc(z_full, 1)

                for tt in range(2):
                    logits(0, tt)
                for head in range(HEADS):
                    p, e = head // 2, head % 2
                    for tt in range(2):
                        unit = (h * HEADS + head) * 2 + tt
                        if head + 1 < HEADS:
                            logits(head + 1, tt)
                        pe.wait_ge(a_ready, unit + 1)
                        if unit >= 2:
                            pe.wait_ge(a_t_ready, unit - 1)
                        for j in range(keys_seen(tt) // P):
                            last = nc.tensor.transpose(acc[tt][:, j * P:(j + 1) * P], beta[:, tt, j * P:(j + 1) * P], ident[:, :])
                        last.then_inc(a_t_full, 1)
                    pe.wait_ge(a_t_ready, (h * HEADS + head) * 2 + 2)
                    if h * HEADS + head >= 2:
                        pe.wait_ge(o_ready, h * HEADS + head - 1)
                    blocks = keys_seen(1) // P
                    for j in range(blocks):
                        q0 = 0 if j < blocks - 1 else P
                        last = nc.tensor.matmul(mid[e][:, q0:HALF], values[:, j, p * P:(p + 1) * P], a_t[:, e, j, q0:HALF],
                                                start=j == 0, stop=j == blocks - 1)
                    last.then_inc(o_full, 1)
                pe.wait_ge(o_ready, (h + 1) * HEADS)
                chunks("out", 1, h, by_token(lambda k, tt: q_t[:, k, tt * P:(tt + 1) * P]))

            def select(l, h):
                pe.wait_ge(h_t_ready, norm_no(l, h, 1, 1) + 1)
                base = BASE["pk", l, h]

                def score(s, i):
                    n = i + PK[l, h]
                    pe.wait_ge(acc_free, i + (base + CREDIT + 1))
                    pe.wait_ge(scores_ready, n + 1)
                    for tt in range(2):
                        for c in range(2):
                            at = tt * 2 * NK + c * NK
                            last = nc.tensor.matmul(mid[s][:, at:at + NK], qs[:, s, c * HALF + tt * P:c * HALF + (tt + 1) * P],
                                                    weights[:, s, CHUNK + c * NK:CHUNK + (c + 1) * NK], start=True, stop=True)
                    last.then_inc(scores_full, 1)

                def project(i, s):
                    pe.wait_ge(weights_in[s], i * 16 + (base // 2 + 1) * 16)
                    pe.wait_ge(acc_free, i * 2 + (base + s + 1))
                    by_channel(s, i).then_inc(acc_full, 1)

                project(0, 0)
                with pe.Fori(0, 3) as i:
                    project(i, 1)
                    score(0, i * 2)
                    pe.wait_ge(weights_in[0], i * 16 + (base // 2 + 2) * 16)
                    pe.wait_ge(acc_free, i * 2 + (base + 3))
                    by_channel(0, i).then_inc(acc_full, 1)
                    score(1, i * 2 + 1)
                project(3, 1)
                score(0, 6)
                score(1, 7)

            def gathered(vs):
                pe.wait_ge(acts_ready, vs + 1)
                if vs:
                    pe.wait_ge(x_peer, vs)
                for c in range(2):
                    nc.tensor.matmul(acc_v[c][:, :], zero_row[0:1, :], zero_wide[0:1, :], start=True, stop=False)
                with pe.Fori(0, BATCHES) as b:
                    for r in range(BATCH):
                        n = (b + vs * BATCHES) * BATCH + (r + 1)
                        pe.wait_ge(v_in[r % VR], (b + vs * BATCHES) * (16 * BATCH // VR) + 16 * (r // VR + 1))
                        pe.wait_ge(diag_ready, n)
                        for c in range(2):
                            last = nc.tensor.matmul(acc_v[c][:, :], diag[:, r, :], v_rows[:, r % VR, c * 512:(c + 1) * 512],
                                                    start=False, stop=False)
                        last.then_inc(v_used, 1)
                for c in range(2):
                    last = nc.tensor.matmul(acc_v[c][:, :], zero_row[0:1, :], zero_wide[0:1, :], start=False, stop=True)
                last.then_inc(y_full, 1)

            for what, *at in ORDER:
                if what == "ada":
                    ada(at[0])
                elif what == "mix":
                    norm(at[0], at[1], 0)
                    conv(at[1]) if at[0] == 0 else attention(at[1])
                elif what == "sel":
                    norm(at[0], at[1], 1)
                    select(*at)
                elif what == "seg" and at[0]:
                    gathered(at[0] - 1)

        @block.scalar
        def _(act):
            steps = Steps(act, act_steps, None)
            act.wait_ge(consts_ready, 1)
            act.wait_ge(cols_in, 16)
            nc.scalar.activation(c_act[:, :], col("c"), ACT.Silu).then_inc(c_silu_ready, 1)

            def tile_norm(n, t):
                steps(nc.scalar.activation(xn[:, :], x[:, t, :], ACT.Square, accum_out=sumsq[:, :]))
                nc.scalar.activation(root[:, :], sumsq[:, :], ACT.Sqrt, scale=1.0 / D, bias=eps_col[:, :]).then_inc(root_ready, 1)
                act.wait_ge(rstd_ready, n + 1)
                nc.scalar.activation(xn[:, :], x[:, t, :], ACT.Copy, scale=rstd[:, :]).then_inc(xn_ready, 1)

            def norm(l, h, which):
                if which:
                    act.wait_ge(acc_free, acc_done("out", l, h))
                elif l == 0:
                    act.wait_ge(x_in, 16)
                act.wait_ge(mod_ready, l + 1)
                for tt in range(2):
                    n = norm_no(l, h, which, tt)
                    t = 2 * h + tt
                    if l and not which:
                        act.wait_ge(x_peer, t + 1)
                    rows_made = half_no(l, h) * 2 + tt * which
                    if rows_made:
                        act.wait_ge(h_rows_ready, rows_made)
                    tile_norm(n, t)
                    for g in range(2):
                        act.wait_ge(xn_t_full, 2 * n + g + 1)
                        for j in range(4):
                            k = 4 * g + j
                            last = nc.scalar.activation(h_t[:, k, tt * P:(tt + 1) * P], mid[g][:, j * P:(j + 1) * P], ACT.Identity,
                                                        scale=mod_cols[:, 2 * which + 1, k:k + 1],
                                                        bias=mod_cols[:, 2 * which, k:k + 1])
                    last.then_inc(h_t_ready, 1)

            def conv(h):
                base = BASE["glu", 0, h]
                with act.Fori(0, 4) as i:
                    for s in range(2):
                        act.wait_ge(acc_full, i * 2 + (base + s + 1))
                        nc.scalar.activation(gate_sig[:, s, :], acc[s][:, HALF:2 * HALF], ACT.Sigmoid,
                                             bias=col("b_in", i * 2 + (KB + s))).then_inc(sig_ready, 1)
                act.wait_ge(centred, h + 1)
                nc.scalar.activation(c_sq[:, :, :], c_t[:, :, :], ACT.Square).then_inc(squared, 1)
                act.wait_ge(var_full, h + 1)
                nc.scalar.activation(ln_rstd, mid[1][:, 0:HALF], ACT.Sqrt, bias=eps_col[:, :]).then_inc(dev_ready, 1)
                act.wait_ge(normed, h + 1)
                for k in range(KB):
                    last = nc.scalar.activation(c_t[:, k, :], c_t[:, k, :], ACT.Silu, scale=col("ln_g", k), bias=col("ln_b", k))
                last.then_inc(silu_ready, 1)

            def attention(h):
                base = BASE["qkv", 1, h]
                act.wait_ge(picks_ready, TILES + 2 * h)
                for kind in range(3):
                    with act.Fori(0, 2) as i:
                        for s in range(2):
                            act.wait_ge(acc_full, i * 2 + (base + 4 * kind + s + 1))
                            two = acc[s][:, :].rearrange("p (c t) -> p c t", c=2)
                            if kind == 0:
                                to = q_t[:, bass.ds(i * 4 + 2 * s, 2), :]
                            elif kind == 1:
                                to = keys_t[:, bass.ds(i * 4 + 2 * s, 2), h * HALF:(h + 1) * HALF]
                            else:
                                to = values[:, 2 * h:2 * h + 2, bass.ds(i * (2 * NC) + s * NC, NC)]
                            nc.scalar.activation(to, two, ACT.Copy).then_inc(acc_free, 1)

                def sigmoids(head, tt):
                    unit = (head + h * HEADS) * 2 + tt
                    n = (2 * h + tt + 1) * P
                    act.wait_ge(z_full, unit + 1)
                    nc.scalar.activation(stay[:, tt, 0:n], zed[tt][:, 0:n], ACT.Sigmoid, scale=-HD ** -0.5)
                    nc.scalar.activation(beta[:, tt, 0:n], zed[tt][:, 0:n], ACT.Sigmoid, scale=HD ** -0.5).then_inc(sigs_ready, 1)

                def head_out(head, p, e, more):
                    for tt in range(2):
                        n = (2 * h + tt + 1) * P
                        act.wait_ge(a_t_full, (head + h * HEADS) * 2 + (tt + 1))
                        nc.scalar.activation(a_t[:, e, 0:n // P, tt * P:(tt + 1) * P],
                                             acc[tt][:, 0:n].rearrange("p (j q) -> p j q", q=P), ACT.Copy).then_inc(a_t_ready, 1)
                        if more:
                            sigmoids(head + 1, tt)
                    act.wait_ge(o_full, head + (h * HEADS + 1))
                    nc.scalar.activation(q_t[e * HD:(e + 1) * HD, bass.ds(p, 1), :],
                                         mid[e][e * HD:(e + 1) * HD, 0:HALF].unsqueeze(1), ACT.Copy).then_inc(o_ready, 1)

                for tt in range(2):
                    sigmoids(0, tt)
                with act.Fori(0, PAIRS - 1) as p:
                    for e in range(2):
                        head_out(p * 2 + e, p, e, True)
                for e in range(2):
                    head_out(HEADS - 2 + e, PAIRS - 1, e, e == 0)

            def select(l, h):
                base = BASE["pk", l, h]
                if half_no(l, h):
                    act.wait_ge(picks_ready, 2 * half_no(l, h))

                def take_q(i, s):
                    act.wait_ge(acc_full, i + (base + 1))
                    nc.scalar.activation(qs[:, s, :], acc[s][:, :], ACT.Copy).then_inc(acc_free, 1)

                def take_scores(i, s):
                    act.wait_ge(scores_full, i + (PK[l, h] + 1))
                    nc.scalar.activation(scores[:, :, bass.ds(i * (2 * NK), 2 * NK)],
                                         mid[s][:, :].rearrange("p (t n) -> p t n", t=2), ACT.Copy).then_inc(scores_ready, 1)

                take_q(0, 0)
                with act.Fori(0, 3) as i:
                    take_q(i * 2 + 1, 1)
                    take_scores(i * 2, 0)
                    take_q(i * 2 + 2, 0)
                    take_scores(i * 2 + 1, 1)
                take_q(7, 1)
                take_scores(6, 0)
                take_scores(7, 1)
                for tt in range(2):
                    j = 2 * half_no(l, h) + tt
                    act.wait_ge(best_ready, j + 1)
                    nc.scalar.activation(pick_gate[:, j % 4, :], pick_gate[:, j % 4, :], ACT.Exp).then_inc(exp_ready, 1)

            def gathered(us, vs):
                if vs is not None:
                    act.wait_ge(acts_ready, vs + 1)
                    with act.Fori(0, BATCHES) as b:
                        for r in range(BATCH):
                            act.wait_ge(v_used, (b + vs * BATCHES) * BATCH + (r + 1))
                            nc.scalar.activation(diag[:, r, :], ident[:, :], ACT.Copy,
                                                 scale=acts[:, vs % 2, bass.ds(b * BATCH + r, 1)]).then_inc(diag_ready, 1)
                if us is not None:
                    act.wait_ge(dots_ready, us + 1)
                    nc.scalar.activation(acts[:, us % 2, :], dots[:, us % 2, :], ACT.Gelu).then_inc(gelu_ready, 1)

            def final():
                for t in range(TILES):
                    act.wait_ge(x_peer, TILES + t + 1)
                    if t:
                        act.wait_ge(out_ready, t)
                    tile_norm(N_NORMS + t, t)

            for what, *at in ORDER:
                if what == "mix":
                    norm(at[0], at[1], 0)
                    conv(at[1]) if at[0] == 0 else attention(at[1])
                elif what == "sel":
                    norm(at[0], at[1], 1)
                    select(*at)
                elif what == "seg":
                    s = at[0]
                    gathered(s if s < JOBS else None, s - 1 if s else None)
                elif what == "final":
                    final()

        @block.vector
        def _(dve):
            steps = Steps(dve, dve_steps, dve_waits_met)
            tt_op, ts_op = nc.vector.tensor_tensor, nc.vector.tensor_scalar
            stt_op = nc.vector.scalar_tensor_tensor
            dve.wait_ge(consts_ready, 1)
            dve.wait_ge(cols_in, 16)

            def reciprocal_root(n):
                dve.wait_ge(root_ready, n + 1)
                nc.vector.reciprocal(rstd[:, :], root[:, :]).then_inc(rstd_ready, 1)

            def ada(l):
                if l == 0:
                    dve.wait_ge(c_silu_ready, 1)
                nc.vector.tensor_copy(c_wide, c_act[:, :].unsqueeze(2).to_broadcast([P, KB, P])).then_inc(c_wide_ready, 1)
                if l:
                    dve.wait_ge(h_t_ready, norm_no(0, 1, 1, 1) + 1)
                base = BASE["ada", l, 0]
                for first, count, rows in ((0, 8, region[:, 0:2 * D]), (8, 12, mod_rows[:, :]), (20, 4, g2_row[:, l, :])):
                    with dve.Fori(0, count // 2) as i:
                        for s in range(2):
                            dve.wait_ge(acc_full, i * 2 + (base + first + s + 1))
                            nc.vector.tensor_copy(rows[:, bass.ds(i * (2 * NC) + s * NC, NC)], acc[s][:, 0:NC]).then_inc(acc_free, 1)
                dve.wait_ge(cols_full, l + 1)
                dve.wait_ge(acc_free, acc_done("ada", l, 0))
                four = mid[0][:, 0:4 * KB].rearrange("p (m k) -> p m k", m=4)
                at = l * KB
                steps(nc.vector.tensor_copy(mod_cols[:, :, :], four))
                for m, gain in ((1, "g_mix"), (3, "g_ffn")):
                    steps(stt_op(out=mod_cols[:, m, :], in0=mod_cols[:, m, :], scalar=1.0, in1=col(gain, at, KB),
                                 op0=ALU.add, op1=ALU.mult))
                if l == 0:
                    dve.wait_ge(b_out_in, 16)
                    steps(tt_op(b_out_row, b_out_row, g1_row, ALU.mult))
                dve.wait_ge(g_ffn_in, 16 * (l + 1))
                stt_op(out=sc2_row, in0=sc2_row, scalar=1.0, in1=g_ffn_row, op0=ALU.add, op1=ALU.mult).then_inc(mod_ready, 1)
                dve.wait_ge(mod_ready, l + 1)

            def norm(l, h, which):
                for tt in range(2):
                    n = norm_no(l, h, which, tt)
                    reciprocal_root(n)
                    if which:
                        j = 2 * half_no(l, h) + tt
                        dve.wait_ge(xn_ready, n + 1)
                        steps(tt_op(h_rows[:, j % 3, :], xn[:, :], sc2_row, ALU.mult))
                        tt_op(h_rows[:, j % 3, :], h_rows[:, j % 3, :], sh2_row, ALU.add).then_inc(h_rows_ready, 1)

            def residual(l, h):
                base = BASE["out", l, h]
                with steps.loop(2, 2) as i:
                    for s in range(2):
                        dve.wait_ge(acc_full, i * 2 + (base + s + 1))
                        at = bass.ds(i * (2 * NC) + s * NC, NC)
                        both = y_tmp[:, :].rearrange("p (t n) -> p t n", t=2)
                        steps(tt_op(both, acc[s][:, :].rearrange("p (t n) -> p t n", t=2),
                                    g1_row[:, at].unsqueeze(1).to_broadcast([P, 2, NC]), ALU.mult))
                        to = x[:, 2 * h:2 * h + 2, at]
                        tt_op(to, to, both, ALU.add).then_inc(acc_free, 1)
                        dve.wait_ge(acc_free, i * 2 + (base + CREDIT + s + 1))

            def conv(h):
                past = u_t[:, :, 0:PAST]
                if h == 0:
                    steps(nc.vector.memset(past, 0.0))
                else:
                    steps(nc.vector.tensor_copy(past, u_t[:, :, HALF:HALF + PAST]))
                dve.wait_ge(xn_ready, norm_no(0, h, 0, 1) + 1)
                for tt in range(2):
                    steps(tt_op(x[:, 2 * h + tt, :], x[:, 2 * h + tt, :], b_out_row, ALU.add))
                base = BASE["glu", 0, h]
                with steps.loop(4, 2 * WIDTH) as i:
                    for s in range(2):
                        c = i * 2 + s
                        dve.wait_ge(acc_full, i * 2 + (base + s + 1))
                        dve.wait_ge(sig_ready, i * 2 + (h * KB + s + 1))
                        row = i * (2 * (PAST + HALF)) + s * (PAST + HALF)
                        to = region[:, bass.ds(i * (2 * HALF) + (2288 + s * HALF), HALF)]
                        stt_op(out=region[:, bass.ds(row + PAST, HALF)], in0=acc[s][:, 0:HALF], scalar=col("b_in", c),
                               in1=gate_sig[:, s, :], op0=ALU.add, op1=ALU.mult).then_inc(acc_free, 1)
                        dve.wait_ge(acc_free, i * 2 + (base + CREDIT + s + 1))
                        for j in range(WIDTH):
                            seen = region[:, bass.ds(row + j, HALF)]
                            tap = col("w_dw", i * (2 * WIDTH) + (s * WIDTH + j))
                            if j == 0:
                                steps(ts_op(to, seen, tap, col("b_dw", c), ALU.mult, ALU.add))
                            else:
                                steps(stt_op(out=to, in0=seen, scalar=tap, in1=to, op0=ALU.mult, op1=ALU.add))
                dve.sem_inc(conv_ready, 1)
                dve.wait_ge(mean_full, h + 1)
                wide = [P, KB, HALF]
                tt_op(c_t, c_t, mid[0][:, 0:HALF].unsqueeze(1).to_broadcast(wide), ALU.subtract).then_inc(centred, 1)
                dve.wait_ge(dev_ready, h + 1)
                steps(nc.vector.reciprocal(ln_rstd, ln_rstd))
                tt_op(c_t, c_t, ln_rstd.unsqueeze(1).to_broadcast(wide), ALU.mult).then_inc(normed, 1)
                residual(0, h)

            def attention(h):
                def unit(head, tt):
                    n = (2 * h + tt + 1) * P
                    dve.wait_ge(sigs_ready, head * 2 + (h * HEADS * 2 + tt + 1))
                    own = slice(n - P, n)
                    steps(tt_op(stay[:, tt, own], stay[:, tt, own], not_past[:, :], ALU.max))
                    steps(tt_op(beta[:, tt, own], beta[:, tt, own], keep_past[:, :], ALU.mult))
                    steps(nc.vector.tensor_tensor_scan(out=stay[:, tt, 0:n][:, ::-1], data0=stay[:, tt, 0:n][:, ::-1],
                                                       data1=stay[:, tt, 0:n][:, ::-1], initial=1.0,
                                                       op0=ALU.mult, op1=ALU.bypass))
                    tt_op(beta[:, tt, 0:n - 1], beta[:, tt, 0:n - 1], stay[:, tt, 1:n], ALU.mult).then_inc(a_ready, 1)

                with steps.loop(PAIRS, 12) as p:
                    for e in range(2):
                        for tt in range(2):
                            unit(p * 2 + e, tt)
                residual(1, h)

            def select(l, h):
                dve.wait_ge(scores_ready, PK[l, h] + 8 + CREDIT)
                for tt in range(2):
                    j = 2 * half_no(l, h) + tt
                    sixteens = [P, 2, TOPK, TOPK]
                    with steps.loop(PH, 27) as head:
                        steps(nc.vector.tensor_copy(list_[:, :, :], scores[:, tt, bass.ds(head * (2 * NK), 2 * NK)].rearrange(
                            "p (c n) -> p c n", c=2)))
                        for c in range(2):
                            steps.apart()
                            steps(nc.vector.max(top[:, c, 0:8], list_[:, c, :]))
                            steps.apart()
                            steps(nc.vector.max_index(top_i[:, c, 0:8], top[:, c, 0:8], list_[:, c, :]))
                            steps.apart()
                            steps(nc.vector.match_replace(out=rest[:, 0:NK], in_to_replace=top[:, c, 0:8],
                                                          in_values=list_[:, c, :], imm_value=LOWEST))
                            steps.apart()
                            steps(nc.vector.max(top[:, c, 8:16], rest[:, 0:NK]))
                            steps.apart()
                            steps(nc.vector.max_index(top_i[:, c, 8:16], top[:, c, 8:16], rest[:, 0:NK]))
                        steps(nc.vector.tensor_copy(top_f[:, :, :], top_i[:, :, :]))
                        steps(tt_op(cand[:, :].rearrange("p (i k) -> p i k", i=TOPK),
                                    top[:, 0, :].unsqueeze(2).to_broadcast([P, TOPK, TOPK]),
                                    top[:, 1, :].unsqueeze(1).to_broadcast([P, TOPK, TOPK]), ALU.add))
                        steps.apart()
                        steps(nc.vector.max(best[:, 0:8], cand[:, :]))
                        steps.apart()
                        steps(nc.vector.max_index(best_i[:, 0:8], best[:, 0:8], cand[:, :]))
                        steps.apart()
                        steps(nc.vector.match_replace(out=rest[:, :], in_to_replace=best[:, 0:8], in_values=cand[:, :],
                                                      imm_value=LOWEST))
                        steps.apart()
                        steps(nc.vector.max(best[:, 8:16], rest[:, :]))
                        steps.apart()
                        steps(nc.vector.max_index(best_i[:, 8:16], best[:, 8:16], rest[:, :]))
                        steps(nc.vector.tensor_copy(best_all[:, bass.ds(head, 1), :], best[:, :].unsqueeze(1)))
                        steps(ts_op(place_i[:, 0, :], best_i[:, :], 4, None, ALU.logical_shift_right))
                        steps(ts_op(place_i[:, 1, :], best_i[:, :], TOPK - 1, None, ALU.bitwise_and))
                        steps(nc.vector.tensor_copy(place_f[:, :, :], place_i[:, :, :]))
                        steps(tt_op(onehot[:, :, :, :], place_f[:, :, :].unsqueeze(3).to_broadcast(sixteens),
                                    iota16[:, :].unsqueeze(1).unsqueeze(1).to_broadcast(sixteens), ALU.is_equal))
                        steps(tt_op(onehot[:, :, :, :], onehot[:, :, :, :],
                                    top_f[:, :, :].unsqueeze(2).to_broadcast(sixteens), ALU.mult))
                        steps(nc.vector.tensor_reduce(best_of[:, :, :], onehot[:, :, :, :], axis=AX.X, op=ALU.add))
                        steps(ts_op(pre_idx[:, :], best_of[:, 0, :], float(NK), float(l * NK * NK), ALU.mult, ALU.add))
                        steps(tt_op(pick_idx[:, j % 4, bass.ds(head * TOPK, TOPK)], pre_idx[:, :], best_of[:, 1, :], ALU.add))
                    gates = pick_gate[:, j % 4, :].rearrange("p (h k) -> p h k", h=PH)
                    tt_op(gates, best_all[:, :, :], best_all[:, :, 0:1].to_broadcast([P, PH, TOPK]), ALU.subtract
                          ).then_inc(best_ready, 1)
                    dve.wait_ge(exp_ready, j + 1)
                    steps(nc.vector.tensor_reduce(gate_sum[:, :], gates, axis=AX.X, op=ALU.add))
                    steps(nc.vector.reciprocal(gate_inv[:, :], gate_sum[:, :]))
                    tt_op(gates, gates, gate_inv[:, :].unsqueeze(2).to_broadcast([P, PH, TOPK]), ALU.mult
                          ).then_inc(picks_ready, 1)

            def gathered(us, vs):
                if us is not None:
                    dve.wait_ge(h_rows_ready, us + 1)
                    with dve.Fori(0, BATCHES) as b:
                        for r in range(BATCH):
                            dve.wait_ge(u_in[r], (b + us * BATCHES) * 16 + 16)
                            stt_op(out=u_rows[:, r, :], in0=u_rows[:, r, :], scalar=1.0, in1=h_rows[:, us % 3, :],
                                   op0=ALU.mult, op1=ALU.mult, accum_out=dots[:, us % 2, bass.ds(b * BATCH + r, 1)]
                                   ).then_inc(u_used, 1)
                    dve.wait_ge(u_used, (us + 1) * PICKS + U_CREDIT)
                    dve.sem_inc(dots_ready, 1)
                    dve.wait_ge(gelu_ready, us + 1)
                    dve.wait_ge(picks_ready, us + 1)
                    tt_op(acts[:, us % 2, :], acts[:, us % 2, :], pick_gate[:, us % 4, :], ALU.mult).then_inc(acts_ready, 1)
                if vs is not None:
                    l, t = vs // TILES, vs % TILES
                    dve.wait_ge(y_full, vs + 1)
                    for c in range(2):
                        half = slice(c * 512, (c + 1) * 512)
                        steps(tt_op(y_tmp[:, :], acc_v[c][:, :], g2_row[:, l, half], ALU.mult))
                        last = tt_op(x[:, t, half], x[:, t, half], y_tmp[:, :], ALU.add)
                        if c:
                            last.then_inc(x_peer, 1)
                        else:
                            steps(last)

            def final():
                dve.wait_ge(final_in, 16)
                for t in range(TILES):
                    reciprocal_root(N_NORMS + t)
                    dve.wait_ge(xn_ready, N_NORMS + t + 1)
                    tt_op(x[:, t, :], xn[:, :], final_row, ALU.mult).then_inc(out_ready, 1)

            for what, *at in ORDER:
                if what == "ada":
                    ada(at[0])
                elif what == "mix":
                    norm(at[0], at[1], 0)
                    conv(at[1]) if at[0] == 0 else attention(at[1])
                elif what == "sel":
                    norm(at[0], at[1], 1)
                    select(*at)
                elif what == "seg":
                    s = at[0]
                    gathered(s if s < JOBS else None, s - 1 if s else None)
                elif what == "final":
                    final()


def kernel(**inputs):
    import numpy as np
    import concourse.bacc as bacc
    from concourse.bass_utils import run_bass_kernel_spmd

    a = {k: np.asarray(v) for k, v in inputs.items()}

    def chunked(w):
        n = w.shape[1]
        return np.ascontiguousarray(w.reshape(KB, P, n // NC, NC).transpose(2, 1, 0, 3)).reshape(n // NC, P, CHUNK)

    def column(v):
        return v.reshape(-1, P).T

    w_in = a["cv_w_in"][0].reshape(D, 2, KB, P).transpose(0, 2, 1, 3).reshape(D, 2 * D)
    arrays = {
        "x": a["x"][0], "w_in": chunked(w_in), "w_out": chunked(a["cv_w_out"][0]),
        "w_qkv": chunked(a["sb_w_qkv"][0]), "w_o": chunked(a["sb_w_o"][0]),
        "b_out": a["cv_b_out"][0], "g_ffn": a["norm_ffn_g"], "final_g": a["final_g"], "ada_b": a["ada_b"],
        "pk_u": a["pk_u"].reshape(DEPTH * NK * NK, D), "pk_v": a["pk_v"].reshape(DEPTH * NK * NK, D),
        "cols": np.concatenate([column(a["c"][0]), column(a["norm_mix_g"].reshape(-1)), column(a["norm_ffn_g"].reshape(-1)),
                                column(a["cv_b_in"][0]),
                                a["cv_w_dw"][0].reshape(WIDTH, KB, P).transpose(2, 1, 0).reshape(P, KB * WIDTH),
                                column(a["cv_b_dw"][0]), column(a["cv_ln_g"][0]), column(a["cv_ln_b"][0])], axis=1),
    }
    for l in range(DEPTH):
        arrays[f"ada{l}"] = chunked(a["ada_w"][l])
        keys = a["pk_keys"][l].transpose(0, 3, 1, 2).reshape(PH, P, 2 * NK)
        arrays[f"pk{l}"] = np.concatenate([chunked(a["pk_w_q"][l]), keys], axis=2)

    nc = bacc.Bacc("TRN2", target_bir_lowering=False, num_devices=1)
    feeds, aps = {}, {}
    for name, array in arrays.items():
        array = np.ascontiguousarray(array)
        feeds[f"in_{name}"] = array
        aps[name] = nc.dram_tensor(f"in_{name}", array.shape, mybir.dt.from_np(array.dtype), kind="ExternalInput").ap()
    out = nc.dram_tensor("out", (SEQ, D), F32, kind="ExternalOutput").ap()
    build(nc, aps, out)
    got = run_bass_kernel_spmd(nc, [feeds], core_ids=[0])
    return got.results[0]["out"].reshape(1, SEQ, D)
```

```python
from contextlib import ExitStack, contextmanager

import concourse.bass as bass
from concourse import mybir

F32 = mybir.dt.float32
I32 = mybir.dt.int32
U32 = mybir.dt.uint32
ALU = mybir.AluOpType
ACT = mybir.ActivationFunctionType
AX = mybir.AxisListType

P = 128
D = 1024
SEQ = 512
DEPTH = 2
KB = D // P
TILES = SEQ // P
HALF = 2 * P
WIDTH = 31
HEADS = 16
HD = D // HEADS
PAIRS = HEADS // 2
PH = 8
NK = 128
TOPK = 16
PICKS = PH * TOPK
EPS = 1e-6
LOWEST = -3.0e38

NC = 256
CHUNK = KB * NC
SLOT = CHUNK + 2 * NK
UR = 8
VR = 4
BATCH = 8
BATCHES = PICKS // BATCH
ROUNDS = 2
ROUND = NK // ROUNDS
GROUP = 8
GROUPS = HALF // GROUP
PER_BATCH = ROUND // BATCHES

COLS = {}
_at = 0
for _name, _n in (("c", KB), ("g_mix", DEPTH * KB), ("g_ffn", DEPTH * KB), ("b_in", 2 * KB), ("w_dw", KB * WIDTH),
                  ("b_dw", KB), ("ln_g", KB), ("ln_b", KB)):
    COLS[_name] = (_at, _n)
    _at += _n
N_COLS = _at

CHAIN = [("ada", 0, 0, 24),
         ("glu", 0, 0, 8), ("out", 0, 0, 4), ("pk", 0, 0, 8),
         ("glu", 0, 1, 8), ("out", 0, 1, 4), ("pk", 0, 1, 8),
         ("ada", 1, 0, 24),
         ("qkv", 1, 0, 12), ("out", 1, 0, 4), ("pk", 1, 0, 8),
         ("qkv", 1, 1, 12), ("out", 1, 1, 4), ("pk", 1, 1, 8)]
BASE = {}
_n = 0
for _s, _l, _h, _k in CHAIN:
    BASE[_s, _l, _h] = _n
    _n += _k
ADA_CHUNKS = 24
ADA_KEPT = 20


class Steps:

    def __init__(self, engine, sem, met):
        self.engine, self.sem, self.met, self.count, self.static = engine, sem, met, 0, 0

    def apart(self):
        self.engine.sem_inc(self.met, 1)

    def __call__(self, instruction):
        instruction.then_inc(self.sem, 1)
        self.count = self.count + 1
        self.static += 1
        self.engine.wait_ge(self.sem, self.count)

    def behind(self, instruction):
        instruction.then_inc(self.sem, 1)
        self.engine.wait_ge(self.sem, self.count)
        self.count = self.count + 1
        self.static += 1

    def settle(self):
        self.engine.wait_ge(self.sem, self.count)

    @contextmanager
    def loop(self, times, per):
        base, static = self.count, self.static
        with self.engine.Fori(0, times) as i:
            self.count = i * per + base
            yield i
            assert self.static - static == per, (self.static - static, per)
        self.count, self.static = base + times * per, static + times * per


def build(nc, a, out):
    with ExitStack() as ctx:
        def sb(name, shape, dt=F32):
            return ctx.enter_context(nc.sbuf_tensor(name, shape, dt))

        def ps(name):
            return ctx.enter_context(nc.psum_tensor(name, [P, 512], F32))

        def sem(name):
            return ctx.enter_context(nc.semaphore(name))

        x = sb("x", [P, TILES, D])
        mod_rows = sb("mod_rows", [P, 3 * D])
        g1_row, sh2_row, sc2_row = (mod_rows[:, i * D:(i + 1) * D] for i in range(3))
        g2_row = sb("g2_row", [P, D])
        u_rows = sb("u_rows", [P, UR, D])
        v_rows = sb("v_rows", [P, VR, D])
        weights = sb("weights", [P, 2, SLOT])
        h_rows = sb("h_rows", [P, 2, D])
        h_t = sb("h_t", [P, KB, HALF])
        scratch = sb("scratch", [P, 2 * D + 10 * NK])
        region = sb("region", [P, ROUND * HALF])
        cols = sb("cols", [P, N_COLS])
        mod_cols = sb("mod_cols", [P, 4, KB])
        c_act = sb("c_act", [P, KB])
        bias_row = sb("bias_row", [1, 2, NC])
        ident = sb("ident", [P, P])
        ones_mean = sb("ones_mean", [P, P])
        one_row = sb("one_row", [1, P])
        zero_row = sb("zero_row", [1, P])
        keep_past = sb("keep_past", [P, P])
        not_past = sb("not_past", [P, P])
        iota16 = sb("iota16", [P, TOPK])
        eps_col = sb("eps_col", [P, 1])
        sumsq = sb("sumsq", [P, 1])
        root = sb("root", [P, 1])
        rstd = sb("rstd", [P, 1])
        iota_keys = sb("iota_keys", [P, NK])
        pick_idx = sb("pick_idx", [P, 2, PICKS], I32)
        pick_gate = sb("pick_gate", [P, 2, 2, PICKS])
        pick_key = sb("pick_key", [P, 2, 2, PICKS])
        idx_now = sb("idx_now", [P, 2, 2, BATCH], I32)
        dots = sb("dots", [P, PICKS])
        acts = sb("acts", [P, PICKS])
        top = sb("top", [P, 2, 2, TOPK])
        top_i = sb("top_i", [P, 2, 2, TOPK], U32)
        top_f = sb("top_f", [P, 2, 2, TOPK])
        best = sb("best", [P, 2, TOPK])
        best_i = sb("best_i", [P, 2, TOPK], U32)
        place_i = sb("place_i", [P, 2, 2, TOPK], U32)
        place_f = sb("place_f", [P, 2, 2, TOPK])
        best_of = sb("best_of", [P, 2, 2, TOPK])
        pre_idx = sb("pre_idx", [P, 2, TOPK])
        best_all = sb("best_all", [P, 2, PH, TOPK])
        gate_sum = sb("gate_sum", [P, PH])
        gate_inv = sb("gate_inv", [P, PH])

        xn = scratch[:, 0:D]
        qs = scratch[:, D:2 * D].rearrange("p (s n) -> p s n", s=2)
        rankings = [scratch[:, 2 * D:], mod_rows[:, D:D + 10 * NK]]
        list_ = [r[:, 0:2 * NK].rearrange("p (c n) -> p c n", c=2) for r in rankings]
        rest = [r[:, 2 * NK:4 * NK] for r in rankings]
        cand = [r[:, 4 * NK:6 * NK] for r in rankings]
        onehot = [r[:, 6 * NK:10 * NK].rearrange("p (c i k) -> p c i k", c=2, i=TOPK) for r in rankings]
        y_tmp = scratch[:, 2 * D:2 * D + 512]
        hot2 = scratch[:, 0:2 * GROUP * NK].rearrange("p (s t n) -> p s t n", s=2, t=GROUP)
        hot1 = scratch[:, 2 * GROUP * NK:2 * GROUP * (NK + ROUND)].rearrange("p (s t n) -> p s t n", s=2, t=GROUP)

        y = mod_rows[:, 0:D]
        pick_t = mod_rows[:, D:D + 3 * HALF].rearrange("p (m t) -> p m t", m=3)
        e_act = mod_rows[:, 2 * D:2 * D + 2 * HALF].rearrange("p (s t) -> p s t", s=2)

        keys_t = region[:, 0:4096].rearrange("p (k t) -> p k t", k=KB)
        values = region[:, 4096:8192].rearrange("p (t n) -> p t n", t=TILES)
        q_t = region[:, 8192:10240].rearrange("p (k t) -> p k t", k=KB)
        beta = region[:, 10240:11264].rearrange("p (t n) -> p t n", t=2)
        stay = region[:, 11264:12288].rearrange("p (t n) -> p t n", t=2)
        a_t = region[:, 12288:14336].rearrange("p (e j q) -> p e j q", e=2, q=HALF)
        scores = region[:, 8192:12288].rearrange("p (t n) -> p t n", t=2)
        PAST = WIDTH - 1
        u_t = region[:, 0:KB * (PAST + HALF)].rearrange("p (k t) -> p k t", k=KB)
        c_t = region[:, 2288:4336].rearrange("p (k t) -> p k t", k=KB)
        c_sq = region[:, 4336:6384].rearrange("p (k t) -> p k t", k=KB)
        gate_sig = region[:, 6384:6896].rearrange("p (s t) -> p s t", s=2)
        ln_rstd = region[:, 6896:7152]
        b_out_row = region[:, 7168:8192]
        sh1_row = region[:, 0:1024]
        sc1_row = region[:, 1024:2048]
        g_ffn_row = region[:, 2048:3072]
        c_wide = region[:, 3072:4096].rearrange("p (k m) -> p k m", k=KB)
        final_row = region[:, 0:1024]

        gates_t = region[:, :].rearrange("p (i t) -> p i t", t=HALF)

        out_e = [ps(f"out_e{i}") for i in range(4)]
        acc = [ps("acc0"), ps("acc1")]
        mid = [ps("mid0"), ps("mid1")]
        zed = out_e[0:2]

        def col(name, i=None, n=1):
            at, size = COLS[name]
            return cols[:, at:at + size] if i is None else cols[:, bass.ds(i + at, n)]

        cols_in, x_in, b_out_in, g_ffn_in, final_in = map(sem, ("cols_in", "x_in", "b_out_in", "g_ffn_in", "final_in"))
        consts_ready = sem("consts_ready")
        weights_in = [sem(f"weights_in{i}") for i in range(2)]
        bias_in = [sem(f"bias_in{i}") for i in range(2)]
        acc_full, acc_free = sem("acc_full"), sem("acc_free")
        c_silu_ready, c_wide_ready, cols_full, mod_ready = map(sem, ("c_silu_ready", "c_wide_ready", "cols_full", "mod_ready"))
        root_ready, rstd_ready, xn_ready, xn_t_full, h_t_ready, h_rows_ready = map(
            sem, ("root_ready", "rstd_ready", "xn_ready", "xn_t_full", "h_t_ready", "h_rows_ready"))
        sig_ready, conv_ready, mean_full, centred, squared, var_full, dev_ready, normed, silu_ready = map(
            sem, ("sig_ready", "conv_ready", "mean_full", "centred", "squared", "var_full", "dev_ready", "normed", "silu_ready"))
        scores_full, scores_ready = map(sem, ("scores_full", "scores_ready"))
        best_ready, exp_ready, picks_ready = map(sem, ("best_ready", "exp_ready", "picks_ready"))
        z_full, sigs_ready, a_ready, a_t_full, a_t_ready, o_full, o_ready = map(
            sem, ("z_full", "sigs_ready", "a_ready", "a_t_full", "a_t_ready", "o_full", "o_ready"))
        idx_staged = sem("idx_staged")
        u_in = [sem(f"u_in{i}") for i in range(UR)]
        v_in = [sem(f"v_in{i}") for i in range(VR)]
        u_used, v_used = sem("u_used"), sem("v_used")
        dots_ready, gelu_ready, acts_ready, x_peer = map(sem, ("dots_ready", "gelu_ready", "acts_ready", "x_peer"))
        utab_in = [sem(f"utab_in{i}") for i in range(2)]
        vtab_in = [sem(f"vtab_in{i}") for i in range(2)]
        picks_t_full, picks_t_ready, hots_ready, gates_full, gates_ready = map(
            sem, ("picks_t_full", "picks_t_ready", "hots_ready", "gates_full", "gates_ready"))
        e_dots_full, e_gelu_ready, e_act_ready, vtab_used, e_out_full = map(
            sem, ("e_dots_full", "e_gelu_ready", "e_act_ready", "vtab_used", "e_out_full"))
        act_steps, dve_steps, pool_steps = sem("act_steps"), sem("dve_steps"), sem("pool_steps")
        pool_waits_met, dve_waits_met = sem("pool_waits_met"), sem("dve_waits_met")
        out_ready, stored = sem("out_ready"), sem("stored")

        CREDIT = 2
        U_CREDIT, V_CREDIT = BATCH, BATCH

        def acc_done(stage, l, h):
            return CREDIT + BASE[stage, l, h] + {s[:3]: s[3] for s in CHAIN}[stage, l, h]

        def half_no(l, h):
            return 2 * l + h

        def norm_no(l, h, which, tt):
            return (half_no(l, h) * 2 + which) * 2 + tt

        N_NORMS = 4 * 2 * DEPTH
        PK = {(l, h): half_no(l, h) * 8 for l in range(DEPTH) for h in range(2)}
        block = ctx.enter_context(nc.Block())

        def dense_no(l, g, i=0):
            return (l * ROUNDS + g) * ROUND + i

        ORDER = [("ada", 0, 0), ("mix", 0, 0), ("sel", 0, 0), ("mix", 0, 1), ("sel", 0, 1), ("peer", 0),
                 ("ada", 1, 0), ("mix", 1, 0), ("sel", 1, 0), ("mix", 1, 1), ("sel", 1, 1), ("peer", 1), ("final",)]

        @block.sync
        def _(sp):
            sp.dma_start(cols[:, :], a["cols"]).then_inc(cols_in, 16)
            src = {("ada", l, 0): a[f"ada{l}"] for l in range(DEPTH)}
            for h in range(2):
                src |= {("glu", 0, h): a["w_in"], ("out", 0, h): a["w_out"], ("qkv", 1, h): a["w_qkv"],
                        ("out", 1, h): a["w_o"], ("pk", 0, h): a["pk0"], ("pk", 1, h): a["pk1"]}
            pk_before = 0

            def tables(l):
                def block_in(i, s, first):
                    n = i + dense_no(l, 0)
                    sp.wait_ge(*((scores_full, PK[l, 1] + 7 + s) if first else (e_dots_full, n - 1)))
                    sp.dma_start(weights[:, s, 0:D], a["u_t"][bass.ds(i + l * NK, 1), :, :].rearrange("a p n -> p (a n)")
                                 ).then_inc(utab_in[s], 16)
                    if not first:
                        sp.wait_ge(vtab_used, n - 1)
                    sp.dma_start(weights[:, s, D:2 * D], a["pk_v"][bass.ds((i + l * NK) * NK, NK), :]).then_inc(vtab_in[s], 16)

                for s in range(2):
                    block_in(s, s, True)
                with sp.Fori(1, NK // 2) as i:
                    for s in range(2):
                        block_in(i * 2 + s, s, False)

            for at, (stage, l, h, count) in enumerate(CHAIN):
                base = BASE[stage, l, h]
                width = SLOT if stage == "pk" else CHUNK
                source = src[stage, l, h]
                before = CHAIN[at - 1][0] if at else None

                def load(i, s, free, value):
                    if free is not None:
                        sp.wait_ge(free, value)
                    sp.dma_start(weights[:, s, 0:width], source[bass.ds(i, 1), :, :].rearrange("a p n -> p (a n)")
                                 ).then_inc(weights_in[s], 16)
                    if stage == "ada":
                        sp.dma_start(bias_row[0:1, s, :], a["ada_b"][l:l + 1, bass.ds(i * NC, NC)]).then_inc(bias_in[s], 16)

                for s in range(2):
                    if before is None:
                        load(s, s, None, 0)
                    elif stage == "ada":
                        load(s, s, vtab_used, dense_no(l, 0, s - 1))
                    elif before == "pk":
                        load(s, s, scores_full, pk_before - 1 + s)
                    else:
                        load(s, s, acc_full, base - 1 + s)
                if stage == "ada":
                    if l == 0:
                        sp.dma_start(x[:, :, :], a["x"].rearrange("(t p) d -> p t d", p=P)).then_inc(x_in, 16)
                        sp.dma_start(b_out_row, a["b_out"].partition_broadcast(P)).then_inc(b_out_in, 16)
                    else:
                        sp.wait_ge(e_act_ready, NK)
                    sp.dma_start(g_ffn_row, a["g_ffn"][l, :].partition_broadcast(P)).then_inc(g_ffn_in, 16)
                with sp.Fori(1, count // 2) as i:
                    for s in range(2):
                        if stage == "pk":
                            load(i * 2 + s, s, scores_full, i * 2 + (PK[l, h] - 1 + s))
                        else:
                            load(i * 2 + s, s, acc_full, i * 2 + (base - 1 + s))
                if stage == "pk":
                    pk_before = PK[l, h] + 8
                if stage == "pk" and h:
                    tables(l)
            sp.wait_ge(e_act_ready, DEPTH * NK)
            sp.dma_start(final_row, a["final_g"].partition_broadcast(P)).then_inc(final_in, 16)
            for t in range(TILES):
                sp.wait_ge(out_ready, t + 1)
                sp.dma_start(out[t * P:(t + 1) * P, :], x[:, t, :]).then_inc(stored, 16)
            sp.wait_ge(stored, 16 * TILES)

        @block.gpsimd
        def _(pool):
            steps = Steps(pool, pool_steps, pool_waits_met)
            steps(nc.gpsimd.memset(ident[:, :], 0.0))
            steps(nc.gpsimd.affine_select(out=ident[:, :], in_=ident[:, :], compare_op=ALU.not_equal, fill=1.0,
                                          base=0, pattern=[[-1, P]], channel_multiplier=1))
            steps(nc.gpsimd.memset(keep_past[:, :], 1.0))
            steps(nc.gpsimd.affine_select(out=keep_past[:, :], in_=keep_past[:, :], compare_op=ALU.is_gt, fill=0.0,
                                          base=0, pattern=[[-1, P]], channel_multiplier=1))
            steps(nc.gpsimd.memset(not_past[:, :], 0.0))
            steps(nc.gpsimd.affine_select(out=not_past[:, :], in_=not_past[:, :], compare_op=ALU.is_gt, fill=1.0,
                                          base=0, pattern=[[-1, P]], channel_multiplier=1))
            steps(nc.gpsimd.iota(iota16[:, :], pattern=[[1, TOPK]], base=0, channel_multiplier=0,
                                 allow_small_or_imprecise_dtypes=True))
            steps(nc.gpsimd.memset(ones_mean[:, :], 1.0 / D))
            steps(nc.gpsimd.memset(one_row[:, :], 1.0))
            steps(nc.gpsimd.memset(zero_row[:, :], 0.0))
            steps(nc.gpsimd.iota(iota_keys[:, :], pattern=[[1, NK]], base=0, channel_multiplier=0,
                                 allow_small_or_imprecise_dtypes=True))
            nc.gpsimd.memset(eps_col[:, :], EPS).then_inc(consts_ready, 1)
            pool.sem_inc(u_used, U_CREDIT)
            pool.sem_inc(v_used, V_CREDIT)

            def stage_indices(q, b, par, dst):
                steps(nc.gpsimd.tensor_copy(idx_now[:, dst, par, :], pick_idx[:, q % 2, bass.ds(b * BATCH, BATCH)]))

            def u_row(q, b, par, r):
                pool.wait_ge(u_used, (b + q * BATCHES) * BATCH + (r + 1 + U_CREDIT - UR))
                steps.apart()
                nc.gpsimd.indirect_dma_start(u_rows[:, r, :], None, a["pk_u"], bass.IndirectOffsetOnAxis(
                    ap=idx_now[:, 0, par, r:r + 1], axis=0)).then_inc(u_in[r], 16)

            def v_row(q, b, par, r):
                pool.wait_ge(v_used, (b + q * BATCHES) * BATCH + (r + 1 + V_CREDIT - VR))
                steps.apart()
                nc.gpsimd.indirect_dma_start(v_rows[:, r % VR, :], None, a["pk_v"], bass.IndirectOffsetOnAxis(
                    ap=idx_now[:, 1, par, r:r + 1], axis=0)).then_inc(v_in[r % VR], 16)

            def indices(q, b, par, dst):
                pool.wait_ge(*((u_used, (b + q * BATCHES) * BATCH + (1 + U_CREDIT - BATCH)) if dst == 0 else
                               (v_used, (b + q * BATCHES) * BATCH + (1 + V_CREDIT - BATCH))))
                steps.apart()
                stage_indices(q, b, par, dst)

            def both(q, b, par, last):
                indices(q, b, par, 1)
                if not last:
                    indices(q, b + 1, 1 - par, 0)
                for r in range(BATCH):
                    if not last:
                        u_row(q, b + 1, 1 - par, r)
                    v_row(q, b, par, r)

            for q in range(2 * DEPTH):
                pool.wait_ge(picks_ready, 4 * (q // 2) + q % 2 + 1)
                indices(q, 0, 0, 0) if q else stage_indices(q, 0, 0, 0)
                for r in range(BATCH):
                    u_row(q, 0, 0, r)
                with steps.loop(BATCHES // 2 - 1, 4) as i:
                    for par in range(2):
                        both(q, i * 2 + par, par, False)
                both(q, BATCHES - 2, 0, False)
                both(q, BATCHES - 1, 1, True)

        @block.tensor
        def _(pe):
            pe.sem_inc(acc_free, CREDIT)
            pe.sem_inc(scores_ready, CREDIT)
            pe.sem_inc(gates_ready, CREDIT)
            pe.wait_ge(consts_ready, 1)

            def chunks(stage, l, h, product):
                base = BASE[stage, l, h]
                count = {c[:3]: c[3] for c in CHAIN}[stage, l, h]
                with pe.Fori(0, count // 2) as i:
                    for s in range(2):
                        pe.wait_ge(weights_in[s], i * 16 + (base // 2 + 1) * 16)
                        pe.wait_ge(acc_free, i * 2 + (base + s + 1))
                        product(s, i).then_inc(acc_full, 1)

            def by_token(lhs):
                def product(s, i):
                    for tt in range(2):
                        for k in range(KB):
                            last = nc.tensor.matmul(acc[s][:, tt * NC:(tt + 1) * NC], lhs(k, tt),
                                                    weights[:, s, k * NC:(k + 1) * NC], start=k == 0, stop=k == KB - 1)
                    return last
                return product

            def by_channel(s, i):
                for c in range(2):
                    for k in range(KB):
                        last = nc.tensor.matmul(acc[s][:, c * HALF:(c + 1) * HALF],
                                                weights[:, s, k * NC + c * P:k * NC + (c + 1) * P], h_t[:, k, :],
                                                start=k == 0, stop=k == KB - 1)
                return last

            def norm(l, h, which):
                for tt in range(2):
                    n = norm_no(l, h, which, tt)
                    pe.wait_ge(xn_ready, n + 1)
                    if n:
                        pe.wait_ge(h_t_ready, n)
                    for g in range(2):
                        for j in range(4):
                            k = 4 * g + j
                            last = nc.tensor.transpose(mid[g][:, j * P:(j + 1) * P], xn[:, k * P:(k + 1) * P], ident[:, :])
                        last.then_inc(xn_t_full, 1)

            def ada(l):
                pe.wait_ge(c_wide_ready, l + 1)

                def product(s, i):
                    for k in range(KB):
                        nc.tensor.matmul(acc[s][:, 0:NC], c_wide[:, k, :], weights[:, s, k * NC:(k + 1) * NC],
                                         start=k == 0, stop=False)
                    pe.wait_ge(bias_in[s], i * 16 + (l * ADA_CHUNKS // 2 + 1) * 16)
                    return nc.tensor.matmul(acc[s][:, 0:NC], one_row[0:1, :], bias_row[0:1, s, :], start=False, stop=True)
                chunks("ada", l, 0, product)
                pe.wait_ge(acc_free, acc_done("ada", l, 0))
                for m, row in enumerate((sh1_row, sc1_row, sh2_row, sc2_row)):
                    for k in range(KB):
                        at = m * KB + k
                        last = nc.tensor.matmul(mid[0][:, at:at + 1], row[0:1, k * P:(k + 1) * P], one_row[0:1, 0:1],
                                                start=True, stop=True)
                last.then_inc(cols_full, 1)

            def conv(h):
                pe.wait_ge(h_t_ready, norm_no(0, h, 0, 1) + 1)
                chunks("glu", 0, h, by_channel)
                pe.wait_ge(conv_ready, h + 1)
                for k in range(KB):
                    last = nc.tensor.matmul(mid[0][:, 0:HALF], ones_mean[:, :], c_t[:, k, :], start=k == 0, stop=k == KB - 1)
                last.then_inc(mean_full, 1)
                pe.wait_ge(squared, h + 1)
                for k in range(KB):
                    last = nc.tensor.matmul(mid[1][:, 0:HALF], ones_mean[:, :], c_sq[:, k, :], start=k == 0, stop=k == KB - 1)
                last.then_inc(var_full, 1)
                pe.wait_ge(silu_ready, h + 1)
                chunks("out", 0, h, by_token(lambda k, tt: c_t[:, k, tt * P:(tt + 1) * P]))

            def attention(h):
                pe.wait_ge(h_t_ready, norm_no(1, h, 0, 1) + 1)
                with pe.Fori(0, 4) as i:
                    for s in range(2):
                        base = BASE["qkv", 1, h]
                        pe.wait_ge(weights_in[s], i * 16 + (base // 2 + 1) * 16)
                        pe.wait_ge(acc_free, i * 2 + (base + s + 1))
                        by_channel(s, i).then_inc(acc_full, 1)
                with pe.Fori(0, 2) as i:
                    for s in range(2):
                        base = BASE["qkv", 1, h] + 8
                        pe.wait_ge(weights_in[s], i * 16 + (base // 2 + 1) * 16)
                        pe.wait_ge(acc_free, i * 2 + (base + s + 1))
                        by_token(lambda k, tt: h_t[:, k, tt * P:(tt + 1) * P])(s, i).then_inc(acc_full, 1)
                pe.wait_ge(acc_free, acc_done("qkv", 1, h))

                def keys_seen(tt):
                    return (2 * h + tt + 1) * P

                def logits(head, tt):
                    p, e = head // 2, head % 2
                    unit = (h * HEADS + head) * 2 + tt
                    if unit >= 2:
                        pe.wait_ge(sigs_ready, unit - 1)
                    nc.tensor.matmul(zed[tt][:, 0:keys_seen(tt)], q_t[e * HD:(e + 1) * HD, p, tt * P:(tt + 1) * P],
                                     keys_t[e * HD:(e + 1) * HD, p, 0:keys_seen(tt)], start=True, stop=True
                                     ).then_inc(z_full, 1)

                for tt in range(2):
                    logits(0, tt)
                for head in range(HEADS):
                    p, e = head // 2, head % 2
                    for tt in range(2):
                        unit = (h * HEADS + head) * 2 + tt
                        if head + 1 < HEADS:
                            logits(head + 1, tt)
                        pe.wait_ge(a_ready, unit + 1)
                        if unit >= 2:
                            pe.wait_ge(a_t_ready, unit - 1)
                        for j in range(keys_seen(tt) // P):
                            last = nc.tensor.transpose(acc[tt][:, j * P:(j + 1) * P], beta[:, tt, j * P:(j + 1) * P], ident[:, :])
                        last.then_inc(a_t_full, 1)
                    pe.wait_ge(a_t_ready, (h * HEADS + head) * 2 + 2)
                    if h * HEADS + head >= 2:
                        pe.wait_ge(o_ready, h * HEADS + head - 1)
                    blocks = keys_seen(1) // P
                    for j in range(blocks):
                        q0 = 0 if j < blocks - 1 else P
                        last = nc.tensor.matmul(mid[e][:, q0:HALF], values[:, j, p * P:(p + 1) * P], a_t[:, e, j, q0:HALF],
                                                start=j == 0, stop=j == blocks - 1)
                    last.then_inc(o_full, 1)
                pe.wait_ge(o_ready, (h + 1) * HEADS)
                chunks("out", 1, h, by_token(lambda k, tt: q_t[:, k, tt * P:(tt + 1) * P]))

            def select(l, h):
                pe.wait_ge(h_t_ready, norm_no(l, h, 1, 1) + 1)
                base = BASE["pk", l, h]

                def score(s, i):
                    n = i + PK[l, h]
                    pe.wait_ge(acc_free, i + (base + CREDIT + 1))
                    pe.wait_ge(scores_ready, n + 1)
                    for tt in range(2):
                        for c in range(2):
                            at = tt * 2 * NK + c * NK
                            last = nc.tensor.matmul(mid[s][:, at:at + NK], qs[:, s, c * HALF + tt * P:c * HALF + (tt + 1) * P],
                                                    weights[:, s, CHUNK + c * NK:CHUNK + (c + 1) * NK], start=True, stop=True)
                    last.then_inc(scores_full, 1)

                def project(i, s):
                    pe.wait_ge(weights_in[s], i * 16 + (base // 2 + 1) * 16)
                    pe.wait_ge(acc_free, i * 2 + (base + s + 1))
                    by_channel(s, i).then_inc(acc_full, 1)

                project(0, 0)
                with pe.Fori(0, 3) as i:
                    project(i, 1)
                    score(0, i * 2)
                    pe.wait_ge(weights_in[0], i * 16 + (base // 2 + 2) * 16)
                    pe.wait_ge(acc_free, i * 2 + (base + 3))
                    by_channel(0, i).then_inc(acc_full, 1)
                    score(1, i * 2 + 1)
                project(3, 1)
                score(0, 6)
                score(1, 7)

            def peer(l):
                pe.wait_ge(picks_ready, 4 * (l + 1))
                for m in range(3):
                    for tt in range(2):
                        src = pick_key[:, tt, m, :] if m < 2 else pick_gate[:, 1, tt, :]
                        at = m * HALF + tt * P
                        last = nc.tensor.transpose(mid[at // 512][:, at % 512:at % 512 + P], src, ident[:, :])
                last.then_inc(picks_t_full, 1)
                pe.wait_ge(picks_t_ready, l + 1)
                for c in range(4):
                    nc.tensor.matmul(out_e[c][:, :], zero_row[0:1, :], zero_row[0:1, 0:1].to_broadcast([1, 512]), start=True, stop=False)
                for g in range(ROUNDS):
                    with pe.Fori(0, GROUPS // 2) as i:
                        for s in range(2):
                            n = i * 2 + ((l * ROUNDS + g) * GROUPS + s)
                            pe.wait_ge(hots_ready, n + 1)
                            pe.wait_ge(gates_ready, n + 1)
                            for t in range(GROUP):
                                last = nc.tensor.matmul(mid[s][:, t * ROUND:(t + 1) * ROUND], hot2[:, s, t, :], hot1[:, s, t, :],
                                                        start=True, stop=True)
                            last.then_inc(gates_full, 1)

                    def u_block(pair, s):
                        pe.wait_ge(utab_in[s], pair * 16 + (dense_no(l, g) // 2 + 1) * 16)
                        n = pair * 2 + (dense_no(l, g) + s)
                        if type(n) is not int or n >= 2:
                            pe.wait_ge(e_gelu_ready, n - 1)
                        for k in range(KB):
                            last = nc.tensor.matmul(acc[s][:, 0:HALF], weights[:, s, k * P:(k + 1) * P], h_t[:, k, :],
                                                    start=k == 0, stop=k == KB - 1)
                        last.then_inc(e_dots_full, 1)

                    def v_block(pair, s):
                        pe.wait_ge(vtab_in[s], pair * 16 + (dense_no(l, g) // 2 + 1) * 16)
                        pe.wait_ge(e_act_ready, pair * 2 + (dense_no(l, g) + s + 1))
                        for tt in range(2):
                            for c in range(2):
                                last = nc.tensor.matmul(out_e[2 * tt + c][:, :], e_act[:, s, tt * P:(tt + 1) * P],
                                                        weights[:, s, D + c * 512:D + (c + 1) * 512], start=False, stop=False)
                        last.then_inc(vtab_used, 1)

                    u_block(0, 0)
                    with pe.Fori(0, ROUND // 2 - 1) as pair:
                        u_block(pair, 1)
                        v_block(pair, 0)
                        u_block(pair + 1, 0)
                        v_block(pair, 1)
                    u_block(ROUND // 2 - 1, 1)
                    v_block(ROUND // 2 - 1, 0)
                    v_block(ROUND // 2 - 1, 1)
                for c in range(4):
                    last = nc.tensor.matmul(out_e[c][:, :], zero_row[0:1, :], zero_row[0:1, 0:1].to_broadcast([1, 512]), start=False, stop=True)
                last.then_inc(e_out_full, 1)

            for what, *at in ORDER:
                if what == "ada":
                    ada(at[0])
                elif what == "mix":
                    norm(at[0], at[1], 0)
                    conv(at[1]) if at[0] == 0 else attention(at[1])
                elif what == "sel":
                    norm(at[0], at[1], 1)
                    select(*at)
                elif what == "peer":
                    peer(at[0])

        @block.scalar
        def _(act):
            steps = Steps(act, act_steps, None)
            act.wait_ge(consts_ready, 1)
            act.wait_ge(cols_in, 16)
            nc.scalar.activation(c_act[:, :], col("c"), ACT.Silu).then_inc(c_silu_ready, 1)

            def tile_norm(n, t):
                steps(nc.scalar.activation(xn[:, :], x[:, t, :], ACT.Square, accum_out=sumsq[:, :]))
                nc.scalar.activation(root[:, :], sumsq[:, :], ACT.Sqrt, scale=1.0 / D, bias=eps_col[:, :]).then_inc(root_ready, 1)
                act.wait_ge(rstd_ready, n + 1)
                nc.scalar.activation(xn[:, :], x[:, t, :], ACT.Copy, scale=rstd[:, :]).then_inc(xn_ready, 1)

            def norm(l, h, which):
                if which:
                    act.wait_ge(acc_free, acc_done("out", l, h))
                elif l == 0:
                    act.wait_ge(x_in, 16)
                else:
                    act.wait_ge(x_peer, 4)
                act.wait_ge(mod_ready, l + 1)
                for tt in range(2):
                    n = norm_no(l, h, which, tt)
                    t = 2 * h + tt
                    rows_made = 2 * l + (tt * which if h == 0 else 2)
                    if rows_made:
                        act.wait_ge(h_rows_ready, rows_made)
                    tile_norm(n, t)
                    for g in range(2):
                        act.wait_ge(xn_t_full, 2 * n + g + 1)
                        for j in range(4):
                            k = 4 * g + j
                            last = nc.scalar.activation(h_t[:, k, tt * P:(tt + 1) * P], mid[g][:, j * P:(j + 1) * P], ACT.Identity,
                                                        scale=mod_cols[:, 2 * which + 1, k:k + 1],
                                                        bias=mod_cols[:, 2 * which, k:k + 1])
                    last.then_inc(h_t_ready, 1)

            def conv(h):
                base = BASE["glu", 0, h]
                with act.Fori(0, 4) as i:
                    for s in range(2):
                        act.wait_ge(acc_full, i * 2 + (base + s + 1))
                        nc.scalar.activation(gate_sig[:, s, :], acc[s][:, HALF:2 * HALF], ACT.Sigmoid,
                                             bias=col("b_in", i * 2 + (KB + s))).then_inc(sig_ready, 1)
                act.wait_ge(centred, h + 1)
                nc.scalar.activation(c_sq[:, :, :], c_t[:, :, :], ACT.Square).then_inc(squared, 1)
                act.wait_ge(var_full, h + 1)
                nc.scalar.activation(ln_rstd, mid[1][:, 0:HALF], ACT.Sqrt, bias=eps_col[:, :]).then_inc(dev_ready, 1)
                act.wait_ge(normed, h + 1)
                for k in range(KB):
                    last = nc.scalar.activation(c_t[:, k, :], c_t[:, k, :], ACT.Silu, scale=col("ln_g", k), bias=col("ln_b", k))
                last.then_inc(silu_ready, 1)

            def attention(h):
                base = BASE["qkv", 1, h]
                act.wait_ge(picks_ready, TILES + 2 * h)
                for kind in range(3):
                    with act.Fori(0, 2) as i:
                        for s in range(2):
                            act.wait_ge(acc_full, i * 2 + (base + 4 * kind + s + 1))
                            two = acc[s][:, :].rearrange("p (c t) -> p c t", c=2)
                            if kind == 0:
                                to = q_t[:, bass.ds(i * 4 + 2 * s, 2), :]
                            elif kind == 1:
                                to = keys_t[:, bass.ds(i * 4 + 2 * s, 2), h * HALF:(h + 1) * HALF]
                            else:
                                to = values[:, 2 * h:2 * h + 2, bass.ds(i * (2 * NC) + s * NC, NC)]
                            nc.scalar.activation(to, two, ACT.Copy).then_inc(acc_free, 1)

                def sigmoids(head, tt):
                    unit = (head + h * HEADS) * 2 + tt
                    n = (2 * h + tt + 1) * P
                    act.wait_ge(z_full, unit + 1)
                    nc.scalar.activation(stay[:, tt, 0:n], zed[tt][:, 0:n], ACT.Sigmoid, scale=-HD ** -0.5)
                    nc.scalar.activation(beta[:, tt, 0:n], zed[tt][:, 0:n], ACT.Sigmoid, scale=HD ** -0.5).then_inc(sigs_ready, 1)

                def head_out(head, p, e, more):
                    for tt in range(2):
                        n = (2 * h + tt + 1) * P
                        act.wait_ge(a_t_full, (head + h * HEADS) * 2 + (tt + 1))
                        nc.scalar.activation(a_t[:, e, 0:n // P, tt * P:(tt + 1) * P],
                                             acc[tt][:, 0:n].rearrange("p (j q) -> p j q", q=P), ACT.Copy).then_inc(a_t_ready, 1)
                        if more:
                            sigmoids(head + 1, tt)
                    act.wait_ge(o_full, head + (h * HEADS + 1))
                    nc.scalar.activation(q_t[e * HD:(e + 1) * HD, bass.ds(p, 1), :],
                                         mid[e][e * HD:(e + 1) * HD, 0:HALF].unsqueeze(1), ACT.Copy).then_inc(o_ready, 1)

                for tt in range(2):
                    sigmoids(0, tt)
                with act.Fori(0, PAIRS - 1) as p:
                    for e in range(2):
                        head_out(p * 2 + e, p, e, True)
                for e in range(2):
                    head_out(HEADS - 2 + e, PAIRS - 1, e, e == 0)

            def select(l, h):
                base = BASE["pk", l, h]
                if half_no(l, h):
                    act.wait_ge(picks_ready, 2 * half_no(l, h))

                def take_q(i, s):
                    act.wait_ge(acc_full, i + (base + 1))
                    nc.scalar.activation(qs[:, s, :], acc[s][:, :], ACT.Copy).then_inc(acc_free, 1)

                def take_scores(i, s):
                    act.wait_ge(scores_full, i + (PK[l, h] + 1))
                    nc.scalar.activation(scores[:, :, bass.ds(i * (2 * NK), 2 * NK)],
                                         mid[s][:, :].rearrange("p (t n) -> p t n", t=2), ACT.Copy).then_inc(scores_ready, 1)

                take_q(0, 0)
                with act.Fori(0, 3) as i:
                    take_q(i * 2 + 1, 1)
                    take_scores(i * 2, 0)
                    take_q(i * 2 + 2, 0)
                    take_scores(i * 2 + 1, 1)
                take_q(7, 1)
                take_scores(6, 0)
                take_scores(7, 1)
                for tt in range(2):
                    j = 2 * half_no(l, h) + tt
                    act.wait_ge(best_ready, j + 1)
                    nc.scalar.activation(pick_gate[:, h, tt, :], pick_gate[:, h, tt, :], ACT.Exp).then_inc(exp_ready, 1)

            def row_gelu(q, b):
                act.wait_ge(dots_ready, b + (q * BATCHES + 1))
                at = bass.ds(b * BATCH, BATCH)
                nc.scalar.activation(acts[:, at], dots[:, at], ACT.Gelu).then_inc(gelu_ready, 1)

            def peer(l):
                act.wait_ge(picks_t_full, l + 1)
                nc.scalar.activation(pick_t[:, 0:2, :].rearrange("p m t -> p (m t)"), mid[0][:, :], ACT.Copy)
                nc.scalar.activation(pick_t[:, 2, :], mid[1][:, 0:HALF], ACT.Copy).then_inc(picks_t_ready, 1)
                for g in range(ROUNDS):
                    q = 2 * l + g
                    with act.Fori(0, GROUPS // 2) as i:
                        for s in range(2):
                            act.wait_ge(gates_full, i * 2 + ((l * ROUNDS + g) * GROUPS + s + 1))
                            nc.scalar.activation(gates_t[:, :, bass.ds(i * (2 * GROUP) + s * GROUP, GROUP)],
                                                 mid[s][:, :].rearrange("p (t i) -> p i t", t=GROUP), ACT.Copy).then_inc(gates_ready, 1)
                    row_gelu(q, 0)

                    def four(b, last):
                        for n in range(PER_BATCH):
                            act.wait_ge(e_dots_full, b * PER_BATCH + (dense_no(l, g) + n + 1))
                            nc.scalar.activation(e_act[:, n % 2, :], acc[n % 2][:, 0:HALF], ACT.Gelu).then_inc(e_gelu_ready, 1)
                        if not last:
                            row_gelu(q, b + 1)

                    with act.Fori(0, BATCHES - 1) as b:
                        four(b, False)
                    four(BATCHES - 1, True)

            def final():
                for t in range(TILES):
                    act.wait_ge(x_peer, 2 * TILES)
                    if t:
                        act.wait_ge(out_ready, t)
                    tile_norm(N_NORMS + t, t)

            for what, *at in ORDER:
                if what == "mix":
                    norm(at[0], at[1], 0)
                    conv(at[1]) if at[0] == 0 else attention(at[1])
                elif what == "sel":
                    norm(at[0], at[1], 1)
                    select(*at)
                elif what == "peer":
                    peer(at[0])
                elif what == "final":
                    final()

        @block.vector
        def _(dve):
            steps = Steps(dve, dve_steps, dve_waits_met)
            tt_op, ts_op = nc.vector.tensor_tensor, nc.vector.tensor_scalar
            stt_op = nc.vector.scalar_tensor_tensor
            dve.wait_ge(consts_ready, 1)
            dve.wait_ge(cols_in, 16)

            def reciprocal_root(n):
                dve.wait_ge(root_ready, n + 1)
                nc.vector.reciprocal(rstd[:, :], root[:, :]).then_inc(rstd_ready, 1)

            def ada(l):
                if l == 0:
                    dve.wait_ge(c_silu_ready, 1)
                nc.vector.tensor_copy(c_wide, c_act[:, :].unsqueeze(2).to_broadcast([P, KB, P])).then_inc(c_wide_ready, 1)
                if l:
                    dve.wait_ge(h_t_ready, norm_no(0, 1, 1, 1) + 1)
                base = BASE["ada", l, 0]
                for first, count, rows in ((0, 8, region[:, 0:2 * D]), (8, 12, mod_rows[:, :]), (20, 4, g2_row[:, :])):
                    with dve.Fori(0, count // 2) as i:
                        for s in range(2):
                            dve.wait_ge(acc_full, i * 2 + (base + first + s + 1))
                            nc.vector.tensor_copy(rows[:, bass.ds(i * (2 * NC) + s * NC, NC)], acc[s][:, 0:NC]).then_inc(acc_free, 1)
                dve.wait_ge(cols_full, l + 1)
                dve.wait_ge(acc_free, acc_done("ada", l, 0))
                four = mid[0][:, 0:4 * KB].rearrange("p (m k) -> p m k", m=4)
                at = l * KB
                steps(nc.vector.tensor_copy(mod_cols[:, :, :], four))
                for m, gain in ((1, "g_mix"), (3, "g_ffn")):
                    steps(stt_op(out=mod_cols[:, m, :], in0=mod_cols[:, m, :], scalar=1.0, in1=col(gain, at, KB),
                                 op0=ALU.add, op1=ALU.mult))
                if l == 0:
                    dve.wait_ge(b_out_in, 16)
                    steps(tt_op(b_out_row, b_out_row, g1_row, ALU.mult))
                dve.wait_ge(g_ffn_in, 16 * (l + 1))
                stt_op(out=sc2_row, in0=sc2_row, scalar=1.0, in1=g_ffn_row, op0=ALU.add, op1=ALU.mult).then_inc(mod_ready, 1)
                dve.wait_ge(mod_ready, l + 1)

            def norm(l, h, which):
                for tt in range(2):
                    n = norm_no(l, h, which, tt)
                    reciprocal_root(n)
                    if which and h == 0:
                        dve.wait_ge(xn_ready, n + 1)
                        steps(tt_op(h_rows[:, tt, :], xn[:, :], sc2_row, ALU.mult))
                        tt_op(h_rows[:, tt, :], h_rows[:, tt, :], sh2_row, ALU.add).then_inc(h_rows_ready, 1)

            def residual(l, h):
                base = BASE["out", l, h]
                with steps.loop(2, 2) as i:
                    for s in range(2):
                        dve.wait_ge(acc_full, i * 2 + (base + s + 1))
                        at = bass.ds(i * (2 * NC) + s * NC, NC)
                        both = y_tmp[:, :].rearrange("p (t n) -> p t n", t=2)
                        steps(tt_op(both, acc[s][:, :].rearrange("p (t n) -> p t n", t=2),
                                    g1_row[:, at].unsqueeze(1).to_broadcast([P, 2, NC]), ALU.mult))
                        to = x[:, 2 * h:2 * h + 2, at]
                        tt_op(to, to, both, ALU.add).then_inc(acc_free, 1)
                        dve.wait_ge(acc_free, i * 2 + (base + CREDIT + s + 1))

            def conv(h):
                past = u_t[:, :, 0:PAST]
                if h == 0:
                    steps(nc.vector.memset(past, 0.0))
                else:
                    steps(nc.vector.tensor_copy(past, u_t[:, :, HALF:HALF + PAST]))
                dve.wait_ge(xn_ready, norm_no(0, h, 0, 1) + 1)
                for tt in range(2):
                    steps(tt_op(x[:, 2 * h + tt, :], x[:, 2 * h + tt, :], b_out_row, ALU.add))
                base = BASE["glu", 0, h]
                with steps.loop(4, 2 * WIDTH) as i:
                    for s in range(2):
                        dve.wait_ge(acc_full, i * 2 + (base + s + 1))
                        dve.wait_ge(sig_ready, i * 2 + (h * KB + s + 1))
                        row = i * (2 * (PAST + HALF)) + (s * (PAST + HALF) + PAST)
                        stt_op(out=region[:, bass.ds(row, HALF)], in0=acc[s][:, 0:HALF], scalar=col("b_in", i * 2 + s),
                               in1=gate_sig[:, s, :], op0=ALU.add, op1=ALU.mult).then_inc(acc_free, 1)
                    dve.wait_ge(acc_free, i * 2 + (base + CREDIT + 2))
                    for j in range(WIDTH):
                        for s in range(2):
                            row = i * (2 * (PAST + HALF)) + s * (PAST + HALF)
                            to = region[:, bass.ds(i * (2 * HALF) + (2288 + s * HALF), HALF)]
                            seen = region[:, bass.ds(row + j, HALF)]
                            tap = col("w_dw", i * (2 * WIDTH) + (s * WIDTH + j))
                            if j == 0:
                                steps.behind(ts_op(to, seen, tap, col("b_dw", i * 2 + s), ALU.mult, ALU.add))
                            else:
                                steps.behind(stt_op(out=to, in0=seen, scalar=tap, in1=to, op0=ALU.mult, op1=ALU.add))
                steps.settle()
                dve.sem_inc(conv_ready, 1)
                dve.wait_ge(mean_full, h + 1)
                wide = [P, KB, HALF]
                tt_op(c_t, c_t, mid[0][:, 0:HALF].unsqueeze(1).to_broadcast(wide), ALU.subtract).then_inc(centred, 1)
                dve.wait_ge(dev_ready, h + 1)
                steps(nc.vector.reciprocal(ln_rstd, ln_rstd))
                tt_op(c_t, c_t, ln_rstd.unsqueeze(1).to_broadcast(wide), ALU.mult).then_inc(normed, 1)
                residual(0, h)

            def attention(h):
                def head_weights(head):
                    keys = [(2 * h + tt + 1) * P for tt in range(2)]
                    for tt, n in enumerate(keys):
                        dve.wait_ge(sigs_ready, head * 2 + (h * HEADS * 2 + tt + 1))
                        own = slice(n - P, n)
                        steps.behind(tt_op(stay[:, tt, own], stay[:, tt, own], not_past[:, :], ALU.max))
                        steps.behind(tt_op(beta[:, tt, own], beta[:, tt, own], keep_past[:, :], ALU.mult))
                    for tt, n in enumerate(keys):
                        steps.behind(nc.vector.tensor_tensor_scan(
                            out=stay[:, tt, 0:n][:, ::-1], data0=stay[:, tt, 0:n][:, ::-1], data1=stay[:, tt, 0:n][:, ::-1],
                            initial=1.0, op0=ALU.mult, op1=ALU.bypass))
                    for tt, n in enumerate(keys):
                        if tt:
                            steps.settle()
                        tt_op(beta[:, tt, 0:n - 1], beta[:, tt, 0:n - 1], stay[:, tt, 1:n], ALU.mult).then_inc(a_ready, 1)

                with steps.loop(PAIRS, 12) as p:
                    for e in range(2):
                        head_weights(p * 2 + e)
                residual(1, h)

            def select(l, h):
                sixteens = [P, 2, TOPK, TOPK]
                if h == 0:
                    dve.wait_ge(h_rows_ready, 2 * l + 2)

                def rank(head):
                    def both(step, *at):
                        for tt in range(2):
                            steps.behind(step(tt, *at))

                    def both_apart(step, *at):
                        for tt in range(2):
                            steps.apart()
                            steps.behind(step(tt, *at))

                    max_, max_index, replace = nc.vector.max, nc.vector.max_index, nc.vector.match_replace
                    copy = nc.vector.tensor_copy
                    both(lambda tt: copy(list_[tt], scores[:, tt, bass.ds(head * (2 * NK), 2 * NK)].rearrange(
                        "p (c n) -> p c n", c=2)))
                    for c in range(2):
                        both_apart(lambda tt: max_(top[:, tt, c, 0:8], list_[tt][:, c, :]))
                        both_apart(lambda tt: max_index(top_i[:, tt, c, 0:8], top[:, tt, c, 0:8], list_[tt][:, c, :]))
                        both_apart(lambda tt: replace(out=rest[tt][:, 0:NK], in_to_replace=top[:, tt, c, 0:8],
                                                      in_values=list_[tt][:, c, :], imm_value=LOWEST))
                        both_apart(lambda tt: max_(top[:, tt, c, 8:16], rest[tt][:, 0:NK]))
                        both_apart(lambda tt: max_index(top_i[:, tt, c, 8:16], top[:, tt, c, 8:16], rest[tt][:, 0:NK]))
                    both(lambda tt: copy(top_f[:, tt, :, :], top_i[:, tt, :, :]))
                    both(lambda tt: tt_op(cand[tt][:, :].rearrange("p (i k) -> p i k", i=TOPK),
                                          top[:, tt, 0, :].unsqueeze(2).to_broadcast([P, TOPK, TOPK]),
                                          top[:, tt, 1, :].unsqueeze(1).to_broadcast([P, TOPK, TOPK]), ALU.add))
                    both_apart(lambda tt: max_(best[:, tt, 0:8], cand[tt]))
                    both_apart(lambda tt: max_index(best_i[:, tt, 0:8], best[:, tt, 0:8], cand[tt]))
                    both_apart(lambda tt: replace(out=rest[tt], in_to_replace=best[:, tt, 0:8], in_values=cand[tt],
                                                  imm_value=LOWEST))
                    both_apart(lambda tt: max_(best[:, tt, 8:16], rest[tt]))
                    both_apart(lambda tt: max_index(best_i[:, tt, 8:16], best[:, tt, 8:16], rest[tt]))
                    both(lambda tt: copy(best_all[:, tt, bass.ds(head, 1), :], best[:, tt, :].unsqueeze(1)))
                    both(lambda tt: ts_op(place_i[:, tt, 0, :], best_i[:, tt, :], 4, None, ALU.logical_shift_right))
                    both(lambda tt: ts_op(place_i[:, tt, 1, :], best_i[:, tt, :], TOPK - 1, None, ALU.bitwise_and))
                    both(lambda tt: copy(place_f[:, tt, :, :], place_i[:, tt, :, :]))
                    both(lambda tt: tt_op(onehot[tt], place_f[:, tt, :, :].unsqueeze(3).to_broadcast(sixteens),
                                          iota16[:, :].unsqueeze(1).unsqueeze(1).to_broadcast(sixteens), ALU.is_equal))
                    both(lambda tt: tt_op(onehot[tt], onehot[tt], top_f[:, tt, :, :].unsqueeze(2).to_broadcast(sixteens),
                                          ALU.mult))
                    both(lambda tt: nc.vector.tensor_reduce(best_of[:, tt, :, :], onehot[tt], axis=AX.X, op=ALU.add))
                    here = bass.ds(head * TOPK, TOPK)
                    if h == 0:
                        both(lambda tt: ts_op(pre_idx[:, tt, :], best_of[:, tt, 0, :], float(NK), float(l * NK * NK),
                                              ALU.mult, ALU.add))
                        both(lambda tt: tt_op(pick_idx[:, tt, here], pre_idx[:, tt, :], best_of[:, tt, 1, :], ALU.add))
                    else:
                        both(lambda tt: copy(pick_key[:, tt, :, here], best_of[:, tt, :, :]))

                with steps.loop(PH, 2 * (27 - h)) as head:
                    dve.wait_ge(scores_ready, head + (PK[l, h] + 1 + CREDIT))
                    rank(head)
                steps.settle()
                for tt in range(2):
                    j = 2 * half_no(l, h) + tt
                    gates = pick_gate[:, h, tt, :].rearrange("p (h k) -> p h k", h=PH)
                    tt_op(gates, best_all[:, tt, :, :], best_all[:, tt, :, 0:1].to_broadcast([P, PH, TOPK]), ALU.subtract
                          ).then_inc(best_ready, 1)
                    dve.wait_ge(exp_ready, j + 1)
                    steps(nc.vector.tensor_reduce(gate_sum[:, :], gates, axis=AX.X, op=ALU.add))
                    steps(nc.vector.reciprocal(gate_inv[:, :], gate_sum[:, :]))
                    tt_op(gates, gates, gate_inv[:, :].unsqueeze(2).to_broadcast([P, PH, TOPK]), ALU.mult
                          ).then_inc(picks_ready, 1)

            def u_dot(q, b, r):
                dve.wait_ge(u_in[r], (b + q * BATCHES) * 16 + 16)
                stt_op(out=u_rows[:, r, :], in0=u_rows[:, r, :], scalar=1.0, in1=h_rows[:, q % 2, :], op0=ALU.mult, op1=ALU.mult,
                       accum_out=dots[:, bass.ds(b * BATCH + r, 1)]).then_inc(u_used, 1)

            def dots_done(q, b):
                dve.wait_ge(u_used, (b + q * BATCHES) * BATCH + (BATCH + U_CREDIT))
                dve.sem_inc(dots_ready, 1)

            def weigh(q, b):
                dve.wait_ge(gelu_ready, b + (q * BATCHES + 1))
                at = bass.ds(b * BATCH, BATCH)
                tt_op(acts[:, at], acts[:, at], pick_gate[:, 0, q % 2, at], ALU.mult).then_inc(acts_ready, 1)
                dve.wait_ge(acts_ready, b + (q * BATCHES + 1))

            def v_add(q, b, r):
                n = (b + q * BATCHES) * BATCH + r
                dve.wait_ge(v_in[r % VR], (b + q * BATCHES) * (16 * BATCH // VR) + 16 * (r // VR + 1))
                dve.wait_ge(v_used, n + V_CREDIT)
                stt_op(out=y[:, :], in0=v_rows[:, r % VR, :], scalar=acts[:, bass.ds(b * BATCH + r, 1)], in1=y[:, :],
                       op0=ALU.mult, op1=ALU.add).then_inc(v_used, 1)

            def add_peer(source, t, c):
                half = slice(c * 512, (c + 1) * 512)
                steps(tt_op(y_tmp[:, :], source, g2_row[:, half], ALU.mult))
                steps(tt_op(x[:, t, half], x[:, t, half], y_tmp[:, :], ALU.add))

            def peer(l):
                dve.wait_ge(picks_t_ready, l + 1)
                for g in range(ROUNDS):
                    q = 2 * l + g
                    with steps.loop(GROUPS // 2, 2) as i:
                        for s in range(2):
                            n = i * 2 + ((l * ROUNDS + g) * GROUPS + s)
                            dve.wait_ge(gates_ready, n + 1)
                            for t in range(GROUP):
                                token = i * (2 * GROUP) + (s * GROUP + t)
                                ts_op(hot2[:, s, t, :], iota_keys[:, :], pick_t[:, 1, bass.ds(token, 1)],
                                      pick_t[:, 2, bass.ds(token, 1)], ALU.is_equal, ALU.mult)
                            wide = [P, GROUP, ROUND]
                            steps(tt_op(hot1[:, s, :, :], iota_keys[:, g * ROUND:(g + 1) * ROUND].unsqueeze(1).to_broadcast(wide),
                                        pick_t[:, 0, bass.ds(i * (2 * GROUP) + s * GROUP, GROUP)].unsqueeze(2).to_broadcast(wide),
                                        ALU.is_equal))
                            dve.sem_inc(hots_ready, 1)
                    dve.wait_ge(gates_ready, (l * ROUNDS + g + 1) * GROUPS + CREDIT)
                    dve.wait_ge(h_rows_ready, q + 1)
                    steps(nc.vector.memset(y[:, :], 0.0))
                    for r in range(BATCH):
                        u_dot(q, 0, r)
                    dots_done(q, 0)

                    def four(b, last):
                        weigh(q, b)
                        for n in range(PER_BATCH):
                            at = b * PER_BATCH + n
                            dve.wait_ge(e_gelu_ready, at + (dense_no(l, g) + 1))
                            tt_op(e_act[:, n % 2, :], e_act[:, n % 2, :],
                                  region[:, bass.ds(b * (PER_BATCH * HALF) + n * HALF, HALF)], ALU.mult).then_inc(e_act_ready, 1)
                            for r in range(n * BATCH // PER_BATCH, (n + 1) * BATCH // PER_BATCH):
                                if not last:
                                    u_dot(q, b + 1, r)
                                v_add(q, b, r)
                        if not last:
                            dots_done(q, b + 1)

                    with dve.Fori(0, BATCHES - 1) as b:
                        four(b, False)
                    four(BATCHES - 1, True)
                    dve.wait_ge(v_used, (q + 1) * PICKS + V_CREDIT)
                    for c in range(2):
                        add_peer(y[:, c * 512:(c + 1) * 512], g, c)
                dve.wait_ge(e_out_full, l + 1)
                for tt in range(2):
                    for c in range(2):
                        add_peer(out_e[2 * tt + c][:, :], 2 + tt, c)
                dve.sem_inc(x_peer, 4)

            def final():
                dve.wait_ge(final_in, 16)
                for t in range(TILES):
                    reciprocal_root(N_NORMS + t)
                    dve.wait_ge(xn_ready, N_NORMS + t + 1)
                    tt_op(x[:, t, :], xn[:, :], final_row, ALU.mult).then_inc(out_ready, 1)

            for what, *at in ORDER:
                if what == "ada":
                    ada(at[0])
                elif what == "mix":
                    norm(at[0], at[1], 0)
                    conv(at[1]) if at[0] == 0 else attention(at[1])
                elif what == "sel":
                    norm(at[0], at[1], 1)
                    select(*at)
                elif what == "peer":
                    peer(at[0])
                elif what == "final":
                    final()


def kernel(**inputs):
    import numpy as np
    import concourse.bacc as bacc
    from concourse.bass_utils import run_bass_kernel_spmd

    a = {k: np.asarray(v) for k, v in inputs.items()}

    def chunked(w):
        n = w.shape[1]
        return np.ascontiguousarray(w.reshape(KB, P, n // NC, NC).transpose(2, 1, 0, 3)).reshape(n // NC, P, CHUNK)

    def column(v):
        return v.reshape(-1, P).T

    w_in = a["cv_w_in"][0].reshape(D, 2, KB, P).transpose(0, 2, 1, 3).reshape(D, 2 * D)
    arrays = {
        "x": a["x"][0], "w_in": chunked(w_in), "w_out": chunked(a["cv_w_out"][0]),
        "w_qkv": chunked(a["sb_w_qkv"][0]), "w_o": chunked(a["sb_w_o"][0]),
        "b_out": a["cv_b_out"][0], "g_ffn": a["norm_ffn_g"], "final_g": a["final_g"], "ada_b": a["ada_b"],
        "pk_u": a["pk_u"].reshape(DEPTH * NK * NK, D), "pk_v": a["pk_v"].reshape(DEPTH * NK * NK, D),
        "cols": np.concatenate([column(a["c"][0]), column(a["norm_mix_g"].reshape(-1)), column(a["norm_ffn_g"].reshape(-1)),
                                column(a["cv_b_in"][0]),
                                a["cv_w_dw"][0].reshape(WIDTH, KB, P).transpose(2, 1, 0).reshape(P, KB * WIDTH),
                                column(a["cv_b_dw"][0]), column(a["cv_ln_g"][0]), column(a["cv_ln_b"][0])], axis=1),
    }
    arrays["u_t"] = a["pk_u"].reshape(DEPTH * NK, NK, KB, P).transpose(0, 3, 2, 1).reshape(DEPTH * NK, P, D)
    for l in range(DEPTH):
        arrays[f"ada{l}"] = chunked(a["ada_w"][l])
        keys = a["pk_keys"][l].transpose(0, 3, 1, 2).reshape(PH, P, 2 * NK)
        arrays[f"pk{l}"] = np.concatenate([chunked(a["pk_w_q"][l]), keys], axis=2)

    nc = bacc.Bacc("TRN2", target_bir_lowering=False, num_devices=1)
    feeds, aps = {}, {}
    for name, array in arrays.items():
        array = np.ascontiguousarray(array)
        feeds[f"in_{name}"] = array
        aps[name] = nc.dram_tensor(f"in_{name}", array.shape, mybir.dt.from_np(array.dtype), kind="ExternalInput").ap()
    out = nc.dram_tensor("out", (SEQ, D), F32, kind="ExternalOutput").ap()
    build(nc, aps, out)
    got = run_bass_kernel_spmd(nc, [feeds], core_ids=[0])
    return got.results[0]["out"].reshape(1, SEQ, D)
```

```python
from contextlib import ExitStack, contextmanager

import concourse.bass as bass
from concourse import mybir

F32 = mybir.dt.float32
I32 = mybir.dt.int32
U32 = mybir.dt.uint32
ALU = mybir.AluOpType
ACT = mybir.ActivationFunctionType
AX = mybir.AxisListType

P = 128
D = 1024
SEQ = 512
DEPTH = 2
KB = D // P
TILES = SEQ // P
HALF = 2 * P
WIDTH = 31
HEADS = 16
HD = D // HEADS
PAIRS = HEADS // 2
PH = 8
NK = 128
TOPK = 16
PICKS = PH * TOPK
EPS = 1e-6
LOWEST = -3.0e38

NC = 256
CHUNK = KB * NC
UR = 8
VR = 4
BATCH = 8
BATCHES = PICKS // BATCH
ROUNDS = 4
ROUND = NK // ROUNDS
GROUPS = ROUND
GROUP = HALF // GROUPS
PER_BATCH = NK // (2 * BATCHES)
EARLY = 4

COLS = {}
_at = 0
for _name, _n in (("c", KB), ("g_mix", DEPTH * KB), ("g_ffn", DEPTH * KB), ("b_in", 2 * KB), ("w_dw", KB * WIDTH),
                  ("b_dw", KB), ("ln_g", KB), ("ln_b", KB)):
    COLS[_name] = (_at, _n)
    _at += _n
N_COLS = _at

CHAIN = [("ada", 0, 0, 12), ("ada", 0, 1, 6),
         ("glu", 0, 0, 8), ("out", 0, 0, 4), ("pk", 0, 0, 8),
         ("ada", 1, 0, 12),
         ("glu", 0, 1, 8), ("out", 0, 1, 4), ("pk", 0, 1, 8),
         ("ada", 1, 1, 12),
         ("qkv", 1, 0, 12), ("out", 1, 0, 4), ("pk", 1, 0, 8),
         ("qkv", 1, 1, 12), ("out", 1, 1, 4), ("pk", 1, 1, 8)]
BASE = {}
_n = 0
for _s, _l, _h, _k in CHAIN:
    BASE[_s, _l, _h] = _n
    _n += _k
ADA_CHUNKS = 6 * D // NC
ADA_PART = ADA_CHUNKS // 2
ASIDE = 6
SH1, SC1, G1, SH2, SC2, G2 = range(0, ADA_CHUNKS, D // NC)


class Steps:

    def __init__(self, engine, sem, met):
        self.engine, self.sem, self.met, self.count, self.static = engine, sem, met, 0, 0

    def apart(self):
        self.engine.sem_inc(self.met, 1)

    def __call__(self, instruction):
        instruction.then_inc(self.sem, 1)
        self.count = self.count + 1
        self.static += 1
        self.engine.wait_ge(self.sem, self.count)

    def behind(self, instruction):
        instruction.then_inc(self.sem, 1)
        self.engine.wait_ge(self.sem, self.count)
        self.count = self.count + 1
        self.static += 1

    def free(self, instruction):
        instruction.then_inc(self.sem, 1)
        self.count = self.count + 1
        self.static += 1

    def settle(self):
        self.engine.wait_ge(self.sem, self.count)

    @contextmanager
    def loop(self, times, per):
        base, static = self.count, self.static
        with self.engine.Fori(0, times) as i:
            self.count = i * per + base
            yield i
            assert self.static - static == per, (self.static - static, per)
        self.count, self.static = base + times * per, static + times * per


assert GROUPS == ROUND and GROUP * ROUND <= 512 and BATCHES % 2 == 0


def build(nc, a, out):
    with ExitStack() as ctx:
        def sb(name, shape, dt=F32):
            return ctx.enter_context(nc.sbuf_tensor(name, shape, dt))

        def ps(name):
            return ctx.enter_context(nc.psum_tensor(name, [P, 512], F32))

        def sem(name):
            return ctx.enter_context(nc.semaphore(name))

        x = sb("x", [P, TILES, D])
        mod_rows = sb("mod_rows", [P, 3 * D])
        g1_row, sh2_row, sc2_row = (mod_rows[:, i * D:(i + 1) * D] for i in range(3))
        g2_row = sb("g2_row", [P, D])
        u_rows = sb("u_rows", [P, UR, D])
        v_rows = sb("v_rows", [P, VR, D])
        weights = sb("weights", [P, 2, CHUNK])
        h_rows = sb("h_rows", [P, 2, D])
        h_t = sb("h_t", [P, KB, HALF])
        scratch = sb("scratch", [P, 2 * D + 10 * NK])
        region = sb("region", [P, 2 * ROUND * HALF])
        cols = sb("cols", [P, N_COLS])
        mod_cols = sb("mod_cols", [P, 4, KB])
        c_act = sb("c_act", [P, KB])
        c_pad = sb("c_pad", [P, KB, 2 * ADA_CHUNKS - 1])
        ada_rows = sb("ada_rows", [ADA_CHUNKS, NC])
        ada_bias = sb("ada_bias", [ADA_CHUNKS, NC])
        ident = sb("ident", [P, P])
        ones_mean = sb("ones_mean", [P, P])
        zero_row = sb("zero_row", [1, P])
        keep_past = sb("keep_past", [P, P])
        not_past = sb("not_past", [P, P])
        iota16 = sb("iota16", [P, TOPK])
        eps_col = sb("eps_col", [P, 1])
        sumsq = sb("sumsq", [P, 2])
        root = sb("root", [P, 2])
        rstd = sb("rstd", [P, 2])
        iota_keys = sb("iota_keys", [P, NK])
        pick_idx = sb("pick_idx", [P, 2, PICKS], I32)
        pick_gate = sb("pick_gate", [P, 2, 2, PICKS])
        pick_key = sb("pick_key", [P, 2, 2, PICKS])
        idx_now = sb("idx_now", [P, 2, 2, BATCH], I32)
        dots = sb("dots", [P, PICKS])
        acts = sb("acts", [P, PICKS])
        top = sb("top", [P, 2, 2, TOPK])
        top_i = sb("top_i", [P, 2, 2, TOPK], U32)
        top_f = sb("top_f", [P, 2, 2, TOPK])
        best = sb("best", [P, 2, TOPK])
        best_i = sb("best_i", [P, 2, TOPK], U32)
        place_i = sb("place_i", [P, 2, 2, TOPK], U32)
        place_f = sb("place_f", [P, 2, 2, TOPK])
        best_of = sb("best_of", [P, 2, 2, TOPK])
        pre_idx = sb("pre_idx", [P, 2, TOPK])
        best_all = sb("best_all", [P, 2, PH, TOPK])
        gate_sum = sb("gate_sum", [P, PH])
        gate_inv = sb("gate_inv", [P, PH])

        xn = scratch[:, 0:D]
        qs = scratch[:, D:2 * D].rearrange("p (s n) -> p s n", s=2)
        rankings = [scratch[:, 2 * D:], mod_rows[:, D:D + 10 * NK]]
        list_ = [r[:, 0:2 * NK].rearrange("p (c n) -> p c n", c=2) for r in rankings]
        rest = [r[:, 2 * NK:4 * NK] for r in rankings]
        cand = [r[:, 4 * NK:6 * NK] for r in rankings]
        onehot = [r[:, 6 * NK:10 * NK].rearrange("p (c i k) -> p c i k", c=2, i=TOPK) for r in rankings]
        y_tmps = scratch[:, 2 * D:3 * D].rearrange("p (c n) -> p c n", c=2)
        y_tmp = scratch[:, 2 * D + 512:3 * D]
        hot2 = scratch[:, 0:2 * GROUP * NK].rearrange("p (s t n) -> p s t n", s=2, t=GROUP)
        hot1 = scratch[:, 2 * GROUP * NK:2 * GROUP * (NK + ROUND)].rearrange("p (s t n) -> p s t n", s=2, t=GROUP)

        y = mod_rows[:, 0:D]
        pick_t = mod_rows[:, D:D + 3 * HALF].rearrange("p (m t) -> p m t", m=3)
        e_act = mod_rows[:, 2 * D:2 * D + 2 * HALF].rearrange("p (s t) -> p s t", s=2)

        aside = ([u_rows[:, i:i + 2, :].rearrange("p r n -> p (r n)") for i in range(0, UR, 2)] +
                 [v_rows[:, i:i + 2, :].rearrange("p r n -> p (r n)") for i in range(0, VR, 2)])[:ASIDE]
        sub_keys = u_rows[:, 0:2 * PH * NK // D, :].rearrange("p r n -> p (r n)")

        keys_t = region[:, 0:4096].rearrange("p (k t) -> p k t", k=KB)
        values = region[:, 4096:8192].rearrange("p (t n) -> p t n", t=TILES)
        q_t = region[:, 8192:10240].rearrange("p (k t) -> p k t", k=KB)
        beta = region[:, 10240:12288].rearrange("p (e t n) -> p e t n", e=2, t=2)
        stay = region[:, 14336:16384].rearrange("p (e t n) -> p e t n", e=2, t=2)
        a_t = region[:, 12288:14336].rearrange("p (e j q) -> p e j q", e=2, q=HALF)
        scores = region[:, 12288:16384].rearrange("p (t n) -> p t n", t=2)
        PAST = WIDTH - 1
        u_t = region[:, 0:KB * (PAST + HALF)].rearrange("p (k t) -> p k t", k=KB)
        c_t = region[:, 2288:4336].rearrange("p (k t) -> p k t", k=KB)
        c_sq = region[:, 4336:6384].rearrange("p (k t) -> p k t", k=KB)
        gate_sig = region[:, 6384:6896].rearrange("p (s t) -> p s t", s=2)
        ln_rstd = region[:, 6896:7152]
        b_out_row = region[:, 7168:8192]
        g_ffn_row = region[:, 15360:16384]
        final_row = region[:, 0:1024]

        gates_t = region[:, :].rearrange("p (g i t) -> p g i t", g=2, t=HALF)

        out_e = [ps(f"out_e{i}") for i in range(4)]
        acc = [ps("acc0"), ps("acc1")]
        mid = [ps("mid0"), ps("mid1")]
        zed = [out_e[0:2], out_e[2:4]]

        def col(name, i=None, n=1):
            at, size = COLS[name]
            return cols[:, at:at + size] if i is None else cols[:, bass.ds(i + at, n)]

        cols_in, x_in, b_out_in, g_ffn_in, final_in, keys_in = map(
            sem, ("cols_in", "x_in", "b_out_in", "g_ffn_in", "final_in", "keys_in"))
        consts_ready = sem("consts_ready")
        weights_in = [sem(f"weights_in{i}") for i in range(2)]
        bias_in = sem("bias_in")
        aside_in = [sem(f"aside_in{i}") for i in range(ASIDE)]
        aside_used = sem("aside_used")
        acc_full, acc_free = sem("acc_full"), sem("acc_free")
        c_silu_ready, c_pad_ready, ada_taken, ada_ready, cols_full, rows_full, mod_ready, rows_ready, rows_done = map(
            sem, ("c_silu_ready", "c_pad_ready", "ada_taken", "ada_ready", "cols_full", "rows_full", "mod_ready",
                  "rows_ready", "rows_done"))
        root_ready, rstd_ready, xn_ready, xn_t_full, h_t_ready, h_rows_ready = map(
            sem, ("root_ready", "rstd_ready", "xn_ready", "xn_t_full", "h_t_ready", "h_rows_ready"))
        sig_ready, conv_ready, mean_full, centred, squared, var_full, dev_ready, normed, silu_ready = map(
            sem, ("sig_ready", "conv_ready", "mean_full", "centred", "squared", "var_full", "dev_ready", "normed", "silu_ready"))
        scores_full, scores_ready = map(sem, ("scores_full", "scores_ready"))
        best_ready, exp_ready, picks_ready = map(sem, ("best_ready", "exp_ready", "picks_ready"))
        z_full, sigs_ready, a_ready, a_t_full, a_t_ready, o_full, o_ready = map(
            sem, ("z_full", "sigs_ready", "a_ready", "a_t_full", "a_t_ready", "o_full", "o_ready"))
        u_in = [sem(f"u_in{i}") for i in range(UR)]
        v_in = [sem(f"v_in{i}") for i in range(VR)]
        u_used, v_used = sem("u_used"), sem("v_used")
        dots_ready, gelu_ready, acts_ready, x_peer = map(sem, ("dots_ready", "gelu_ready", "acts_ready", "x_peer"))
        utab_in = [sem(f"utab_in{i}") for i in range(2)]
        vtab_in = [sem(f"vtab_in{i}") for i in range(2)]
        picks_t_full, picks_t_ready, hots_ready, gates_full, gates_ready = map(
            sem, ("picks_t_full", "picks_t_ready", "hots_ready", "gates_full", "gates_ready"))
        e_dots_full, e_gelu_ready, e_act_ready, vtab_used, e_out_full = map(
            sem, ("e_dots_full", "e_gelu_ready", "e_act_ready", "vtab_used", "e_out_full"))
        act_steps, dve_steps, pool_steps = sem("act_steps"), sem("dve_steps"), sem("pool_steps")
        pool_waits_met, dve_waits_met = sem("pool_waits_met"), sem("dve_waits_met")
        out_ready, stored = sem("out_ready"), sem("stored")

        CREDIT = 2
        U_CREDIT, V_CREDIT = BATCH, BATCH

        def acc_done(stage, l, h):
            return CREDIT + BASE[stage, l, h] + {s[:3]: s[3] for s in CHAIN}[stage, l, h]

        def half_no(l, h):
            return 2 * l + h

        def norm_no(l, h, which, tt):
            return (half_no(l, h) * 2 + which) * 2 + tt

        N_NORMS = 4 * 2 * DEPTH
        PK = {(l, h): half_no(l, h) * 8 for l in range(DEPTH) for h in range(2)}
        halves = [slice(0, KB // 2), slice(KB // 2, KB)]
        block = ctx.enter_context(nc.Block())

        def dense_no(l, g, i=0):
            return (l * ROUNDS + g) * ROUND + i

        ORDER = [("ada", 0, 0), ("ada", 0, 1), ("mix", 0, 0), ("sel", 0, 0), ("ada", 1, 0), ("mix", 0, 1),
                 ("sel", 0, 1), ("ada", 1, 1), ("peer", 0),
                 ("mix", 1, 0), ("sel", 1, 0), ("mix", 1, 1), ("sel", 1, 1), ("peer", 1), ("final",)]

        @block.sync
        def _(sp):
            sp.dma_start(cols[:, :], a["cols"]).then_inc(cols_in, 16)
            src = {("ada", l, part): a[f"ada{l}"][part * ADA_PART:(part + 1) * ADA_PART] for l in range(DEPTH) for part in range(2)}
            for h in range(2):
                src |= {("glu", 0, h): a["w_in"], ("out", 0, h): a["w_out"], ("qkv", 1, h): a["w_qkv"],
                        ("out", 1, h): a["w_o"], ("pk", 0, h): a["pk0"], ("pk", 1, h): a["pk1"]}

            def tables(l, before):
                def block_in(i, s, first):
                    n = i + dense_no(l, 0)
                    sp.wait_ge(*((acc_full, before - 1 + s) if first else (e_dots_full, n - 1)))
                    sp.dma_start(weights[:, s, 0:D], a["u_t"][bass.ds(i + l * NK, 1), :, :].rearrange("a p n -> p (a n)")
                                 ).then_inc(utab_in[s], 16)
                    if not first:
                        sp.wait_ge(vtab_used, n - 1)
                    sp.dma_start(weights[:, s, D:2 * D], a["pk_v"][bass.ds((i + l * NK) * NK, NK), :]).then_inc(vtab_in[s], 16)

                for s in range(2):
                    block_in(s, s, True)
                with sp.Fori(1, NK // 2) as i:
                    for s in range(2):
                        block_in(i * 2 + s, s, False)

            for at, (stage, l, h, count) in enumerate(CHAIN):
                base = BASE[stage, l, h]
                source = src[stage, l, h]
                before = CHAIN[at - 1][0] if at else None

                def load(i, s, free, value):
                    if free is not None:
                        sp.wait_ge(free, value)
                    sp.dma_start(weights[:, s, :], source[bass.ds(i, 1), :, :].rearrange("a p n -> p (a n)")
                                 ).then_inc(weights_in[s], 16)

                for s in range(2):
                    if before is None:
                        load(s, s, None, 0)
                    elif stage == "qkv" and h == 0:
                        load(s, s, vtab_used, l * NK - 1 + s)
                    else:
                        load(s, s, acc_full, base - 1 + s)
                if stage == "pk" and h == 0:
                    sp.wait_ge(*((u_used, 2 * l * PICKS + U_CREDIT) if l else (aside_used, 1)))
                    sp.dma_start(sub_keys, a[f"keys{l}"]).then_inc(keys_in, 16)
                if stage == "ada" and h == 0:
                    if l:
                        sp.wait_ge(ada_ready, l)
                    sp.dma_start(ada_bias[:, :], a["ada_b"][l, :].rearrange("(i n) -> i n", n=NC)).then_inc(bias_in, 16)
                    if l == 0:
                        sp.dma_start(x[:, :, :], a["x"].rearrange("(t p) d -> p t d", p=P)).then_inc(x_in, 16)
                        sp.dma_start(b_out_row, a["b_out"].partition_broadcast(P)).then_inc(b_out_in, 16)
                if (stage, h) == ("ada", 0) and l == 0 or (stage, h) == ("qkv", 0):
                    if l:
                        sp.wait_ge(e_act_ready, l * NK)
                    sp.dma_start(g_ffn_row, a["g_ffn"][l, :].partition_broadcast(P)).then_inc(g_ffn_in, 16)
                if at == 0:
                    for i in range(2, count):
                        if i % 2 == 0:
                            n = i // 2 - 1
                            sp.dma_start(aside[n], a["ada0"][ADA_CHUNKS - ASIDE + n, :, :]).then_inc(aside_in[n], 16)
                        load(i, i % 2, acc_full, i - 1)
                    n = ASIDE - 1
                    sp.dma_start(aside[n], a["ada0"][ADA_CHUNKS - 1, :, :]).then_inc(aside_in[n], 16)
                    continue
                with sp.Fori(1, count // 2) as i:
                    for s in range(2):
                        load(i * 2 + s, s, acc_full, i * 2 + (base - 1 + s))
                if (stage, l, h) in (("ada", 1, 1), ("pk", 1, 1)):
                    tables(0 if stage == "ada" else 1, base + count)
            sp.wait_ge(e_act_ready, DEPTH * NK)
            sp.dma_start(final_row, a["final_g"].partition_broadcast(P)).then_inc(final_in, 16)
            for t in range(TILES):
                sp.wait_ge(out_ready, t + 1)
                sp.dma_start(out[t * P:(t + 1) * P, :], x[:, t, :]).then_inc(stored, 16)
            sp.wait_ge(stored, 16 * TILES)

        @block.gpsimd
        def _(pool):
            steps = Steps(pool, pool_steps, pool_waits_met)
            steps(nc.gpsimd.memset(ident[:, :], 0.0))
            steps(nc.gpsimd.affine_select(out=ident[:, :], in_=ident[:, :], compare_op=ALU.not_equal, fill=1.0,
                                          base=0, pattern=[[-1, P]], channel_multiplier=1))
            steps(nc.gpsimd.memset(keep_past[:, :], 1.0))
            steps(nc.gpsimd.affine_select(out=keep_past[:, :], in_=keep_past[:, :], compare_op=ALU.is_gt, fill=0.0,
                                          base=0, pattern=[[-1, P]], channel_multiplier=1))
            steps(nc.gpsimd.memset(not_past[:, :], 0.0))
            steps(nc.gpsimd.affine_select(out=not_past[:, :], in_=not_past[:, :], compare_op=ALU.is_gt, fill=1.0,
                                          base=0, pattern=[[-1, P]], channel_multiplier=1))
            steps(nc.gpsimd.iota(iota16[:, :], pattern=[[1, TOPK]], base=0, channel_multiplier=0,
                                 allow_small_or_imprecise_dtypes=True))
            steps(nc.gpsimd.memset(ones_mean[:, :], 1.0 / D))
            steps(nc.gpsimd.memset(zero_row[:, :], 0.0))
            steps(nc.gpsimd.iota(iota_keys[:, :], pattern=[[1, NK]], base=0, channel_multiplier=0,
                                 allow_small_or_imprecise_dtypes=True))
            nc.gpsimd.memset(eps_col[:, :], EPS).then_inc(consts_ready, 1)
            pool.sem_inc(u_used, U_CREDIT)
            pool.sem_inc(v_used, V_CREDIT)

            def stage_indices(q, b, par, dst):
                steps(nc.gpsimd.tensor_copy(idx_now[:, dst, par, :], pick_idx[:, q % 2, bass.ds(b * BATCH, BATCH)]))

            def u_row(q, b, par, r):
                pool.wait_ge(u_used, (b + q * BATCHES) * BATCH + (r + 1 + U_CREDIT - UR))
                steps.apart()
                nc.gpsimd.indirect_dma_start(u_rows[:, r, :], None, a["pk_u"], bass.IndirectOffsetOnAxis(
                    ap=idx_now[:, 0, par, r:r + 1], axis=0)).then_inc(u_in[r], 16)

            def v_row(q, b, par, r):
                pool.wait_ge(v_used, (b + q * BATCHES) * BATCH + (r + 1 + V_CREDIT - VR))
                steps.apart()
                nc.gpsimd.indirect_dma_start(v_rows[:, r % VR, :], None, a["pk_v"], bass.IndirectOffsetOnAxis(
                    ap=idx_now[:, 1, par, r:r + 1], axis=0)).then_inc(v_in[r % VR], 16)

            def indices(q, b, par, dst):
                pool.wait_ge(*((u_used, (b + q * BATCHES) * BATCH + (1 + U_CREDIT - BATCH)) if dst == 0 else
                               (v_used, (b + q * BATCHES) * BATCH + (1 + V_CREDIT - BATCH))))
                steps.apart()
                stage_indices(q, b, par, dst)

            def both(q, b, par, after):
                indices(q, b, par, 1)
                if after:
                    indices(*after, 1 - par, 0)
                for r in range(BATCH):
                    if after:
                        u_row(*after, 1 - par, r)
                    v_row(q, b, par, r)

            for q in range(2 * DEPTH):
                if q % 2 == 0:
                    pool.wait_ge(picks_ready, 2 * q + 2)
                    pool.wait_ge(scores_full, PK[q // 2, 1] + 8)
                    indices(q, 0, 0, 0) if q else stage_indices(q, 0, 0, 0)
                    for r in range(BATCH):
                        u_row(q, 0, 0, r)
                with steps.loop(BATCHES // 2 - 1, 4) as i:
                    for par in range(2):
                        both(q, i * 2 + par, par, (q, i * 2 + (par + 1)))
                both(q, BATCHES - 2, 0, (q, BATCHES - 1))
                both(q, BATCHES - 1, 1, (q + 1, 0) if q % 2 == 0 else None)

        @block.tensor
        def _(pe):
            pe.sem_inc(acc_free, CREDIT)
            pe.sem_inc(scores_ready, CREDIT)
            pe.sem_inc(gates_ready, CREDIT)
            pe.wait_ge(consts_ready, 1)

            def chunks(stage, l, h, product):
                base = BASE[stage, l, h]
                count = {c[:3]: c[3] for c in CHAIN}[stage, l, h]
                with pe.Fori(0, count // 2) as i:
                    for s in range(2):
                        pe.wait_ge(weights_in[s], i * 16 + (base // 2 + 1) * 16)
                        pe.wait_ge(acc_free, i * 2 + (base + s + 1))
                        product(s, i).then_inc(acc_full, 1)

            def by_token(lhs):
                def product(s, i):
                    for tt in range(2):
                        for k in range(KB):
                            last = nc.tensor.matmul(acc[s][:, tt * NC:(tt + 1) * NC], lhs(k, tt),
                                                    weights[:, s, k * NC:(k + 1) * NC], start=k == 0, stop=k == KB - 1)
                    return last
                return product

            def by_channel(s, i):
                for c in range(2):
                    for k in range(KB):
                        last = nc.tensor.matmul(acc[s][:, c * HALF:(c + 1) * HALF],
                                                weights[:, s, k * NC + c * P:k * NC + (c + 1) * P], h_t[:, k, :],
                                                start=k == 0, stop=k == KB - 1)
                return last

            def norm(l, h, which):
                for tt in range(2):
                    n = norm_no(l, h, which, tt)
                    pe.wait_ge(xn_ready, n + 1)
                    if n:
                        pe.wait_ge(h_t_ready, n)
                    for g in range(2):
                        for j in range(4):
                            k = 4 * g + j
                            last = nc.tensor.transpose(mid[g][:, j * P:(j + 1) * P], xn[:, k * P:(k + 1) * P], ident[:, :])
                        last.then_inc(xn_t_full, 1)

            def ada(l, part):
                pe.wait_ge(c_pad_ready, 1)
                base = BASE["ada", l, part]
                if l and part == 0:
                    pe.wait_ge(rows_ready, 8 * l)
                in_chain = ADA_PART - (ASIDE if (l, part) == (0, 1) else 0)
                for i in range(ADA_PART):
                    n = part * ADA_PART + i
                    if i < in_chain:
                        pe.wait_ge(weights_in[i % 2], (base + i) // 2 * 16 + 16)
                        chunk = weights[:, i % 2, :]
                    else:
                        pe.wait_ge(aside_in[i - in_chain], 16)
                        chunk = aside[i - in_chain]
                    window = ADA_CHUNKS - 1 - n
                    for k in range(KB):
                        last = nc.tensor.matmul(out_e[0][0:ADA_CHUNKS, 0:NC], c_pad[:, k, window:window + ADA_CHUNKS],
                                                chunk[:, k * NC:(k + 1) * NC], start=n + k == 0,
                                                stop=n == ADA_CHUNKS - 1 and k == KB - 1)
                    if i < in_chain:
                        last.then_inc(acc_full, 1)
                    elif n == ADA_CHUNKS - 1:
                        last.then_inc(aside_used, 1)
                pe.wait_ge(acc_free, base + CREDIT)
                pe.sem_inc(acc_free, in_chain)

            def spread_columns(l):
                pe.wait_ge(ada_ready, l + 1)
                for c in range(2):
                    last = nc.tensor.matmul(mid[0][:, c * ADA_CHUNKS:(c + 1) * ADA_CHUNKS], ada_rows[:, c * P:(c + 1) * P],
                                            ident[0:ADA_CHUNKS, 0:ADA_CHUNKS], start=True, stop=True)
                last.then_inc(cols_full, 1)

            def spread_rows(l):
                if l:
                    pe.wait_ge(x_peer, 4 * l)
                for m, first in enumerate((G1, SH2, SC2, G2)):
                    for c in range(D // NC):
                        if m >= 2 and c % 2 == 0:
                            pe.wait_ge(rows_ready, 8 * l + 2 * (m - 2) + c // 2 + 1)
                        pick = ident[0:ADA_CHUNKS, first + c:first + c + 1].to_broadcast([ADA_CHUNKS, P])
                        last = nc.tensor.matmul(out_e[2 * (m % 2) + c // 2][:, c % 2 * NC:(c % 2 + 1) * NC], pick, ada_rows[:, :],
                                                start=True, stop=True)
                        if c % 2:
                            last.then_inc(rows_full, 1)

            def conv(h):
                pe.wait_ge(h_t_ready, norm_no(0, h, 0, 1) + 1)
                base = BASE["glu", 0, h]
                pairs = KB // 2
                for i in range(pairs + 1):
                    if i < pairs:
                        for s in range(2):
                            pe.wait_ge(weights_in[s], (base // 2 + i + 1) * 16)
                            pe.wait_ge(acc_free, base + 2 * i + s + 1)
                            by_channel(s, i).then_inc(acc_full, 1)
                    if i:
                        pe.wait_ge(conv_ready, h * pairs + i)
                        for k in (2 * i - 2, 2 * i - 1):
                            last = nc.tensor.matmul(mid[0][:, 0:HALF], ones_mean[:, :], c_t[:, k, :], start=k == 0, stop=k == KB - 1)
                last.then_inc(mean_full, 1)
                for k in range(KB):
                    if k % (KB // 2) == 0:
                        pe.wait_ge(squared, 2 * h + k // (KB // 2) + 1)
                    last = nc.tensor.matmul(mid[1][:, 0:HALF], ones_mean[:, :], c_sq[:, k, :], start=k == 0, stop=k == KB - 1)
                last.then_inc(var_full, 1)
                pe.wait_ge(silu_ready, h + 1)
                chunks("out", 0, h, by_token(lambda k, tt: c_t[:, k, tt * P:(tt + 1) * P]))

            def attention(h):
                pe.wait_ge(h_t_ready, norm_no(1, h, 0, 1) + 1)
                with pe.Fori(0, 4) as i:
                    for s in range(2):
                        base = BASE["qkv", 1, h]
                        pe.wait_ge(weights_in[s], i * 16 + (base // 2 + 1) * 16)
                        pe.wait_ge(acc_free, i * 2 + (base + s + 1))
                        by_channel(s, i).then_inc(acc_full, 1)
                with pe.Fori(0, 2) as i:
                    for s in range(2):
                        base = BASE["qkv", 1, h] + 8
                        pe.wait_ge(weights_in[s], i * 16 + (base // 2 + 1) * 16)
                        pe.wait_ge(acc_free, i * 2 + (base + s + 1))
                        by_token(lambda k, tt: h_t[:, k, tt * P:(tt + 1) * P])(s, i).then_inc(acc_full, 1)
                pe.wait_ge(rows_done, DEPTH)
                pe.wait_ge(acc_free, acc_done("qkv", 1, h))

                def keys_seen(tt):
                    return (2 * h + tt + 1) * P

                def logits(head, tt):
                    p, e = head // 2, head % 2
                    unit = (h * HEADS + head) * 2 + tt
                    if unit >= 4:
                        pe.wait_ge(sigs_ready, unit - 3)
                    nc.tensor.matmul(zed[e][tt][:, 0:keys_seen(tt)], q_t[e * HD:(e + 1) * HD, p, tt * P:(tt + 1) * P],
                                     keys_t[e * HD:(e + 1) * HD, p, 0:keys_seen(tt)], start=True, stop=True
                                     ).then_inc(z_full, 1)

                for tt in range(2):
                    logits(0, tt)
                for head in range(HEADS):
                    p, e = head // 2, head % 2
                    for tt in range(2):
                        if head + 1 < HEADS:
                            logits(head + 1, tt)
                    for tt in range(2):
                        unit = (h * HEADS + head) * 2 + tt
                        pe.wait_ge(a_ready, unit + 1)
                        if unit >= 2:
                            pe.wait_ge(a_t_ready, unit - 1)
                        for j in range(keys_seen(tt) // P):
                            last = nc.tensor.transpose(acc[tt][:, j * P:(j + 1) * P], beta[:, e, tt, j * P:(j + 1) * P], ident[:, :])
                        last.then_inc(a_t_full, 1)
                    pe.wait_ge(a_t_ready, (h * HEADS + head) * 2 + 2)
                    if h * HEADS + head >= 2:
                        pe.wait_ge(o_ready, h * HEADS + head - 1)
                    blocks = keys_seen(1) // P
                    for j in range(blocks):
                        q0 = 0 if j < blocks - 1 else P
                        last = nc.tensor.matmul(mid[e][:, q0:HALF], values[:, j, p * P:(p + 1) * P], a_t[:, e, j, q0:HALF],
                                                start=j == 0, stop=j == blocks - 1)
                    last.then_inc(o_full, 1)
                pe.wait_ge(o_ready, (h + 1) * HEADS)
                chunks("out", 1, h, by_token(lambda k, tt: q_t[:, k, tt * P:(tt + 1) * P]))

            def select(l, h):
                pe.wait_ge(h_t_ready, norm_no(l, h, 1, 1) + 1)
                base = BASE["pk", l, h]
                pe.wait_ge(keys_in, 16 * (l + 1))

                def score(s, i):
                    n = i + PK[l, h]
                    pe.wait_ge(acc_free, i + (base + CREDIT + 1))
                    pe.wait_ge(scores_ready, n + 1)
                    for tt in range(2):
                        for c in range(2):
                            at = tt * 2 * NK + c * NK
                            last = nc.tensor.matmul(mid[s][:, at:at + NK], qs[:, s, c * HALF + tt * P:c * HALF + (tt + 1) * P],
                                                    sub_keys[:, bass.ds(i * (2 * NK) + c * NK, NK)], start=True, stop=True)
                    last.then_inc(scores_full, 1)

                def project(i, s):
                    pe.wait_ge(weights_in[s], i * 16 + (base // 2 + 1) * 16)
                    pe.wait_ge(acc_free, i * 2 + (base + s + 1))
                    by_channel(s, i).then_inc(acc_full, 1)

                project(0, 0)
                with pe.Fori(0, 3) as i:
                    project(i, 1)
                    score(0, i * 2)
                    pe.wait_ge(weights_in[0], i * 16 + (base // 2 + 2) * 16)
                    pe.wait_ge(acc_free, i * 2 + (base + 3))
                    by_channel(0, i).then_inc(acc_full, 1)
                    score(1, i * 2 + 1)
                project(3, 1)
                score(0, 6)
                score(1, 7)

            def peer(l):
                pe.wait_ge(picks_ready, 4 * (l + 1))
                pe.wait_ge(mod_ready, 2)
                for m in range(3):
                    for tt in range(2):
                        src = pick_key[:, tt, m, :] if m < 2 else pick_gate[:, 1, tt, :]
                        at = m * HALF + tt * P
                        last = nc.tensor.transpose(mid[at // 512][:, at % 512:at % 512 + P], src, ident[:, :])
                last.then_inc(picks_t_full, 1)
                pe.wait_ge(picks_t_ready, l + 1)
                pe.wait_ge(ada_taken, 2)
                for c in range(4):
                    nc.tensor.matmul(out_e[c][:, :], zero_row[0:1, :], zero_row[0:1, 0:1].to_broadcast([1, 512]), start=True, stop=False)

                def gates_group(i, s):
                    n = i * 2 + (l * ROUNDS * GROUPS + s)
                    pe.wait_ge(hots_ready, n + 1)
                    pe.wait_ge(gates_ready, n + 1)
                    for t in range(GROUP):
                        last = nc.tensor.matmul(mid[s][:, t * ROUND:(t + 1) * ROUND], hot2[:, s, t, :], hot1[:, s, t, :],
                                                start=True, stop=True)
                    last.then_inc(gates_full, 1)

                def u_block(pair, s):
                    pe.wait_ge(utab_in[s], pair * 16 + (dense_no(l, 0) // 2 + 1) * 16)
                    n = pair * 2 + (dense_no(l, 0) + s)
                    if type(n) is not int or n >= 2:
                        pe.wait_ge(e_gelu_ready, n - 1)
                    for k in range(KB):
                        last = nc.tensor.matmul(acc[s][:, 0:HALF], weights[:, s, k * P:(k + 1) * P], h_t[:, k, :],
                                                start=k == 0, stop=k == KB - 1)
                    last.then_inc(e_dots_full, 1)

                def v_block(pair, s):
                    pe.wait_ge(vtab_in[s], pair * 16 + (dense_no(l, 0) // 2 + 1) * 16)
                    pe.wait_ge(e_act_ready, pair * 2 + (dense_no(l, 0) + s + 1))
                    for tt in range(2):
                        for c in range(2):
                            last = nc.tensor.matmul(out_e[2 * tt + c][:, :], e_act[:, s, tt * P:(tt + 1) * P],
                                                    weights[:, s, D + c * 512:D + (c + 1) * 512], start=False, stop=False)
                    last.then_inc(vtab_used, 1)

                u_block(0, 0)
                with pe.Fori(0, GROUPS // 2) as i:
                    for s in range(2):
                        gates_group(i, s)
                with pe.Fori(0, (ROUNDS - 1) * ROUND // 2) as pair:
                    for s in range(2):
                        u_block(pair + s, 1 - s)
                        gates_group(pair + GROUPS // 2, s)
                        v_block(pair, s)
                with pe.Fori((ROUNDS - 1) * ROUND // 2, NK // 2 - 1) as pair:
                    for s in range(2):
                        u_block(pair + s, 1 - s)
                        v_block(pair, s)
                u_block(NK // 2 - 1, 1)
                v_block(NK // 2 - 1, 0)
                v_block(NK // 2 - 1, 1)
                for c in range(4):
                    last = nc.tensor.matmul(out_e[c][:, :], zero_row[0:1, :], zero_row[0:1, 0:1].to_broadcast([1, 512]), start=False, stop=True)
                last.then_inc(e_out_full, 1)

            for what, *at in ORDER:
                if what == "ada":
                    ada(*at)
                    if at[1]:
                        spread_columns(at[0])
                elif what == "mix":
                    norm(at[0], at[1], 0)
                    if at[1] == 0:
                        spread_rows(at[0])
                    conv(at[1]) if at[0] == 0 else attention(at[1])
                elif what == "sel":
                    norm(at[0], at[1], 1)
                    select(*at)
                elif what == "peer":
                    peer(at[0])

        @block.scalar
        def _(act):
            steps = Steps(act, act_steps, None)
            act.wait_ge(consts_ready, 1)
            act.wait_ge(cols_in, 16)
            nc.scalar.activation(c_act[:, :], col("c"), ACT.Silu).then_inc(c_silu_ready, 1)

            def roots(n, t, xn_free):
                if xn_free:
                    act.wait_ge(*xn_free)
                for tt in range(2):
                    steps(nc.scalar.activation(xn[:, :], x[:, t + tt, :], ACT.Square, accum_out=sumsq[:, tt:tt + 1]))
                nc.scalar.activation(root[:, :], sumsq[:, :], ACT.Sqrt, scale=1.0 / D, bias=eps_col[:, :]).then_inc(root_ready, 1)
                act.wait_ge(rstd_ready, n + 1)

            def scaled(t):
                nc.scalar.activation(xn[:, :], x[:, t, :], ACT.Copy, scale=rstd[:, t % 2:t % 2 + 1]).then_inc(xn_ready, 1)

            def norm(l, h, which):
                if which:
                    act.wait_ge(acc_free, acc_done("out", l, h))
                elif l == 0:
                    act.wait_ge(x_in, 16)
                else:
                    act.wait_ge(x_peer, 2 + 2 * h)
                act.wait_ge(mod_ready, l + 1)
                for tt in range(2):
                    n = norm_no(l, h, which, tt)
                    rows_made = 2 * l + (tt * which if h == 0 else 2)
                    if tt == 0:
                        roots(n // 2, 2 * h, (h_rows_ready, rows_made) if rows_made else None)
                    elif rows_made:
                        act.wait_ge(h_rows_ready, rows_made)
                    scaled(2 * h + tt)
                    for g in range(2):
                        act.wait_ge(xn_t_full, 2 * n + g + 1)
                        for j in range(4):
                            k = 4 * g + j
                            last = nc.scalar.activation(h_t[:, k, tt * P:(tt + 1) * P], mid[g][:, j * P:(j + 1) * P], ACT.Identity,
                                                        scale=mod_cols[:, 2 * which + 1, k:k + 1],
                                                        bias=mod_cols[:, 2 * which, k:k + 1])
                    last.then_inc(h_t_ready, 1)

            def conv(h):
                base = BASE["glu", 0, h]
                with act.Fori(0, 4) as i:
                    for s in range(2):
                        act.wait_ge(acc_full, i * 2 + (base + s + 1))
                        nc.scalar.activation(gate_sig[:, s, :], acc[s][:, HALF:2 * HALF], ACT.Sigmoid,
                                             bias=col("b_in", i * 2 + (KB + s))).then_inc(sig_ready, 1)
                for n, blocks in enumerate(halves):
                    act.wait_ge(centred, 2 * h + n + 1)
                    nc.scalar.activation(c_sq[:, blocks, :], c_t[:, blocks, :], ACT.Square).then_inc(squared, 1)
                act.wait_ge(var_full, h + 1)
                nc.scalar.activation(ln_rstd, mid[1][:, 0:HALF], ACT.Sqrt, bias=eps_col[:, :]).then_inc(dev_ready, 1)
                for k in range(KB):
                    if k % (KB // 2) == 0:
                        act.wait_ge(normed, 2 * h + k // (KB // 2) + 1)
                    last = nc.scalar.activation(c_t[:, k, :], c_t[:, k, :], ACT.Silu, scale=col("ln_g", k), bias=col("ln_b", k))
                last.then_inc(silu_ready, 1)

            def attention(h):
                base = BASE["qkv", 1, h]
                for kind in range(3):
                    with act.Fori(0, 2) as i:
                        for s in range(2):
                            act.wait_ge(acc_full, i * 2 + (base + 4 * kind + s + 1))
                            two = acc[s][:, :].rearrange("p (c t) -> p c t", c=2)
                            if kind == 0:
                                to = q_t[:, bass.ds(i * 4 + 2 * s, 2), :]
                            elif kind == 1:
                                to = keys_t[:, bass.ds(i * 4 + 2 * s, 2), h * HALF:(h + 1) * HALF]
                            else:
                                to = values[:, 2 * h:2 * h + 2, bass.ds(i * (2 * NC) + s * NC, NC)]
                            nc.scalar.activation(to, two, ACT.Copy).then_inc(acc_free, 1)

                if h:
                    exps(1, 0)
                act.wait_ge(picks_ready, TILES + 2 * h)

                def sigmoids(head, e):
                    for tt in range(2):
                        n = (2 * h + tt + 1) * P
                        act.wait_ge(z_full, (head + h * HEADS) * 2 + (tt + 1))
                        for to, sign in ((stay, -1), (beta, 1)):
                            last = nc.scalar.activation(to[:, e, tt, 0:n], zed[e][tt][:, 0:n], ACT.Sigmoid, scale=sign * HD ** -0.5)
                        last.then_inc(sigs_ready, 1)

                def head_out(head, p, e, more):
                    if more:
                        sigmoids(head + 1, 1 - e)
                    for tt in range(2):
                        n = (2 * h + tt + 1) * P
                        act.wait_ge(a_t_full, (head + h * HEADS) * 2 + (tt + 1))
                        nc.scalar.activation(a_t[:, e, 0:n // P, tt * P:(tt + 1) * P],
                                             acc[tt][:, 0:n].rearrange("p (j q) -> p j q", q=P), ACT.Copy).then_inc(a_t_ready, 1)
                    act.wait_ge(o_full, head + (h * HEADS + 1))
                    nc.scalar.activation(q_t[e * HD:(e + 1) * HD, bass.ds(p, 1), :],
                                         mid[e][e * HD:(e + 1) * HD, 0:HALF].unsqueeze(1), ACT.Copy).then_inc(o_ready, 1)

                sigmoids(0, 0)
                with act.Fori(0, PAIRS - 1) as p:
                    for e in range(2):
                        head_out(p * 2 + e, p, e, True)
                for e in range(2):
                    head_out(HEADS - 2 + e, PAIRS - 1, e, e == 0)

            def select(l, h):
                base = BASE["pk", l, h]
                if half_no(l, h):
                    act.wait_ge(picks_ready, 2 * half_no(l, h))

                def take_q(i, s):
                    act.wait_ge(acc_full, i + (base + 1))
                    nc.scalar.activation(qs[:, s, :], acc[s][:, :], ACT.Copy).then_inc(acc_free, 1)

                def take_scores(i, s):
                    act.wait_ge(scores_full, i + (PK[l, h] + 1))
                    nc.scalar.activation(scores[:, :, bass.ds(i * (2 * NK), 2 * NK)],
                                         mid[s][:, :].rearrange("p (t n) -> p t n", t=2), ACT.Copy).then_inc(scores_ready, 1)

                take_q(0, 0)
                with act.Fori(0, 3) as i:
                    take_q(i * 2 + 1, 1)
                    take_scores(i * 2, 0)
                    take_q(i * 2 + 2, 0)
                    take_scores(i * 2 + 1, 1)
                take_q(7, 1)
                take_scores(6, 0)
                take_scores(7, 1)

            def exps(l, h):
                for tt in range(2):
                    j = 2 * half_no(l, h) + tt
                    act.wait_ge(best_ready, j + 1)
                    nc.scalar.activation(pick_gate[:, h, tt, :], pick_gate[:, h, tt, :], ACT.Exp).then_inc(exp_ready, 1)

            def row_gelu(q, b):
                act.wait_ge(dots_ready, b + (q * BATCHES + 1))
                at = bass.ds(b * BATCH, BATCH)
                nc.scalar.activation(acts[:, at], dots[:, at], ACT.Gelu).then_inc(gelu_ready, 1)

            def peer(l):
                act.wait_ge(picks_t_full, l + 1)
                nc.scalar.activation(pick_t[:, 0:2, :].rearrange("p m t -> p (m t)"), mid[0][:, :], ACT.Copy)
                nc.scalar.activation(pick_t[:, 2, :], mid[1][:, 0:HALF], ACT.Copy).then_inc(picks_t_ready, 1)

                def take_gates(g, i, s):
                    act.wait_ge(gates_full, i * 2 + ((l * ROUNDS + g) * GROUPS + s + 1))
                    nc.scalar.activation(gates_t[:, g % 2, :, bass.ds(i * (2 * GROUP) + s * GROUP, GROUP)],
                                         mid[s][:, 0:GROUP * ROUND].rearrange("p (t i) -> p i t", t=GROUP), ACT.Copy
                                         ).then_inc(gates_ready, 1)

                with act.Fori(0, GROUPS // 2) as i:
                    for s in range(2):
                        take_gates(0, i, s)
                row_gelu(2 * l, 0)
                for g in range(ROUNDS):
                    q, first = 2 * l + g // 2, g % 2 * (BATCHES // 2)
                    if g:
                        act.wait_ge(e_act_ready, dense_no(l, g))

                    def blocks(b):
                        for n in range(PER_BATCH):
                            act.wait_ge(e_dots_full, b * PER_BATCH + (dense_no(l, g) + n + 1))
                            nc.scalar.activation(e_act[:, n % 2, :], acc[n % 2][:, 0:HALF], ACT.Gelu).then_inc(e_gelu_ready, 1)
                            if g + 1 < ROUNDS:
                                take_gates(g + 1, b * (PER_BATCH // 2) + n // 2, n % 2)

                    if g % 2 == 0:
                        with act.Fori(0, BATCHES // 2) as b:
                            blocks(b)
                            row_gelu(q, b + 1)
                    else:
                        with act.Fori(0, BATCHES // 2 - 1) as b:
                            blocks(b)
                            row_gelu(q, b + (first + 1))
                        blocks(BATCHES // 2 - 1)
                        if q % 2 == 0:
                            row_gelu(q + 1, 0)

            def final():
                for t in range(TILES):
                    act.wait_ge(x_peer, 2 * TILES - (2 if t < 2 else 0))
                    if t % 2 == 0:
                        roots((N_NORMS + t) // 2, t, (out_ready, t) if t else None)
                    else:
                        act.wait_ge(out_ready, t)
                    scaled(t)

            def ada(l):
                act.wait_ge(*((acc_full, BASE["ada", l, 1] + ADA_PART) if l else (aside_used, 1)))
                nc.scalar.activation(ada_rows[:, :], out_e[0][0:ADA_CHUNKS, 0:NC], ACT.Copy).then_inc(ada_taken, 1)

            for what, *at in ORDER:
                if what == "ada" and at[1]:
                    ada(at[0])
                elif what == "mix":
                    norm(at[0], at[1], 0)
                    if at == [0, 1]:
                        exps(0, 0)
                    conv(at[1]) if at[0] == 0 else attention(at[1])
                elif what == "sel":
                    norm(at[0], at[1], 1)
                    select(*at)
                    if at[1]:
                        exps(*at)
                elif what == "peer":
                    peer(at[0])
                elif what == "final":
                    final()

        @block.vector
        def _(dve):
            steps = Steps(dve, dve_steps, dve_waits_met)
            tt_op, ts_op = nc.vector.tensor_tensor, nc.vector.tensor_scalar
            stt_op = nc.vector.scalar_tensor_tensor
            dve.wait_ge(consts_ready, 1)
            dve.wait_ge(cols_in, 16)

            def reciprocal_root(n):
                dve.wait_ge(root_ready, n + 1)
                nc.vector.reciprocal(rstd[:, :], root[:, :]).then_inc(rstd_ready, 1)

            def ada(l):
                if l == 0:
                    dve.wait_ge(c_silu_ready, 1)
                    steps(nc.vector.memset(c_pad[:, :, :], 0.0))
                    nc.vector.tensor_copy(c_pad[:, :, ADA_CHUNKS - 1:ADA_CHUNKS], c_act[:, :].unsqueeze(2)).then_inc(c_pad_ready, 1)
                dve.wait_ge(ada_taken, l + 1)
                dve.wait_ge(bias_in, 16 * (l + 1))
                tt_op(ada_rows[:, :], ada_rows[:, :], ada_bias[:, :], ALU.add).then_inc(ada_ready, 1)

            def spread_columns(l):
                dve.wait_ge(cols_full, l + 1)
                columns = mid[0][:, 0:2 * ADA_CHUNKS].rearrange("p (c m k) -> p m k c", c=2, m=6)
                for to, m in ((0, 0), (2, 3)):
                    for r in range(2):
                        steps(nc.vector.tensor_copy(mod_cols[:, to + r, :].rearrange("p (k c) -> p k c", c=2), columns[:, m + r]))
                at = l * KB
                steps(stt_op(out=mod_cols[:, 1, :], in0=mod_cols[:, 1, :], scalar=1.0, in1=col("g_mix", at, KB),
                             op0=ALU.add, op1=ALU.mult))
                stt_op(out=mod_cols[:, 3, :], in0=mod_cols[:, 3, :], scalar=1.0, in1=col("g_ffn", at, KB),
                       op0=ALU.add, op1=ALU.mult).then_inc(mod_ready, 1)

            def spread_rows(l):
                rows = [g1_row, sh2_row, sc2_row, g2_row]
                for i in range(8):
                    dve.wait_ge(rows_full, 8 * l + i + 1)
                    nc.vector.tensor_copy(rows[i // 2][:, i % 2 * 512:(i % 2 + 1) * 512], out_e[i % 4][:, :]).then_inc(rows_ready, 1)
                dve.wait_ge(rows_ready, 8 * (l + 1))
                if l == 0:
                    dve.wait_ge(b_out_in, 16)
                    steps(tt_op(b_out_row, b_out_row, g1_row, ALU.mult))
                dve.wait_ge(g_ffn_in, 16 * (l + 1))
                stt_op(out=sc2_row, in0=sc2_row, scalar=1.0, in1=g_ffn_row, op0=ALU.add, op1=ALU.mult).then_inc(rows_done, 1)
                dve.wait_ge(rows_done, l + 1)

            def norm(l, h, which):
                reciprocal_root(norm_no(l, h, which, 0) // 2)
                if which and h == 0:
                    for tt in range(2):
                        n = norm_no(l, h, which, tt)
                        dve.wait_ge(xn_ready, n + 1)
                        steps(tt_op(h_rows[:, tt, :], xn[:, :], sc2_row, ALU.mult))
                        tt_op(h_rows[:, tt, :], h_rows[:, tt, :], sh2_row, ALU.add).then_inc(h_rows_ready, 1)

            def residual(l, h):
                base = BASE["out", l, h]
                with steps.loop(2, 2) as i:
                    for s in range(2):
                        dve.wait_ge(acc_full, i * 2 + (base + s + 1))
                        at = bass.ds(i * (2 * NC) + s * NC, NC)
                        both = y_tmp[:, :].rearrange("p (t n) -> p t n", t=2)
                        steps(tt_op(both, acc[s][:, :].rearrange("p (t n) -> p t n", t=2),
                                    g1_row[:, at].unsqueeze(1).to_broadcast([P, 2, NC]), ALU.mult))
                        to = x[:, 2 * h:2 * h + 2, at]
                        tt_op(to, to, both, ALU.add).then_inc(acc_free, 1)
                        dve.wait_ge(acc_free, i * 2 + (base + CREDIT + s + 1))

            def conv(h):
                past = u_t[:, :, 0:PAST]
                if h == 0:
                    steps(nc.vector.memset(past, 0.0))
                else:
                    steps(nc.vector.tensor_copy(past, u_t[:, :, HALF:HALF + PAST]))
                dve.wait_ge(xn_ready, norm_no(0, h, 0, 1) + 1)
                for tt in range(2):
                    steps(tt_op(x[:, 2 * h + tt, :], x[:, 2 * h + tt, :], b_out_row, ALU.add))
                base = BASE["glu", 0, h]
                with steps.loop(4, 2 * WIDTH) as i:
                    for s in range(2):
                        dve.wait_ge(acc_full, i * 2 + (base + s + 1))
                        dve.wait_ge(sig_ready, i * 2 + (h * KB + s + 1))
                        row = i * (2 * (PAST + HALF)) + (s * (PAST + HALF) + PAST)
                        stt_op(out=region[:, bass.ds(row, HALF)], in0=acc[s][:, 0:HALF], scalar=col("b_in", i * 2 + s),
                               in1=gate_sig[:, s, :], op0=ALU.add, op1=ALU.mult).then_inc(acc_free, 1)
                    dve.wait_ge(acc_free, i * 2 + (base + CREDIT + 2))
                    for j in range(WIDTH):
                        for s in range(2):
                            row = i * (2 * (PAST + HALF)) + s * (PAST + HALF)
                            to = region[:, bass.ds(i * (2 * HALF) + (2288 + s * HALF), HALF)]
                            seen = region[:, bass.ds(row + j, HALF)]
                            tap = col("w_dw", i * (2 * WIDTH) + (s * WIDTH + j))
                            if j == 0:
                                steps.behind(ts_op(to, seen, tap, col("b_dw", i * 2 + s), ALU.mult, ALU.add))
                            else:
                                step = steps if (j, s) == (WIDTH - 1, 1) else steps.behind
                                step(stt_op(out=to, in0=seen, scalar=tap, in1=to, op0=ALU.mult, op1=ALU.add))
                    dve.sem_inc(conv_ready, 1)
                dve.wait_ge(mean_full, h + 1)
                wide = [P, KB // 2, HALF]
                for blocks in halves:
                    tt_op(c_t[:, blocks, :], c_t[:, blocks, :], mid[0][:, 0:HALF].unsqueeze(1).to_broadcast(wide), ALU.subtract
                          ).then_inc(centred, 1)
                dve.wait_ge(dev_ready, h + 1)
                steps(nc.vector.reciprocal(ln_rstd, ln_rstd))
                for blocks in halves:
                    tt_op(c_t[:, blocks, :], c_t[:, blocks, :], ln_rstd.unsqueeze(1).to_broadcast(wide), ALU.mult
                          ).then_inc(normed, 1)
                residual(0, h)

            def attention(h):
                def head_weights(head, e):
                    keys = [(2 * h + tt + 1) * P for tt in range(2)]
                    for tt, n in enumerate(keys):
                        dve.wait_ge(sigs_ready, head * 2 + (h * HEADS * 2 + tt + 1))
                        own = slice(n - P, n)
                        steps.behind(tt_op(stay[:, e, tt, own], stay[:, e, tt, own], not_past[:, :], ALU.max))
                        steps.behind(tt_op(beta[:, e, tt, own], beta[:, e, tt, own], keep_past[:, :], ALU.mult))
                    for tt, n in enumerate(keys):
                        steps.behind(nc.vector.tensor_tensor_scan(
                            out=stay[:, e, tt, 0:n][:, ::-1], data0=stay[:, e, tt, 0:n][:, ::-1], data1=stay[:, e, tt, 0:n][:, ::-1],
                            initial=1.0, op0=ALU.mult, op1=ALU.bypass))
                    for tt, n in enumerate(keys):
                        if tt:
                            steps.settle()
                        tt_op(beta[:, e, tt, 0:n - 1], beta[:, e, tt, 0:n - 1], stay[:, e, tt, 1:n], ALU.mult).then_inc(a_ready, 1)

                with steps.loop(PAIRS, 12) as p:
                    for e in range(2):
                        head_weights(p * 2 + e, e)
                residual(1, h)

            def select(l, h):
                sixteens = [P, 2, TOPK, TOPK]
                if h == 0:
                    dve.wait_ge(h_rows_ready, 2 * l + 2)

                def rank(head):
                    def both(step, *at):
                        for tt in range(2):
                            steps.behind(step(tt, *at))

                    def both_apart(step, *at):
                        for tt in range(2):
                            steps.apart()
                            steps.behind(step(tt, *at))

                    max_, max_index, replace = nc.vector.max, nc.vector.max_index, nc.vector.match_replace
                    copy = nc.vector.tensor_copy
                    both(lambda tt: copy(list_[tt], scores[:, tt, bass.ds(head * (2 * NK), 2 * NK)].rearrange(
                        "p (c n) -> p c n", c=2)))
                    for c in range(2):
                        both_apart(lambda tt: max_(top[:, tt, c, 0:8], list_[tt][:, c, :]))
                        both_apart(lambda tt: max_index(top_i[:, tt, c, 0:8], top[:, tt, c, 0:8], list_[tt][:, c, :]))
                        both_apart(lambda tt: replace(out=rest[tt][:, 0:NK], in_to_replace=top[:, tt, c, 0:8],
                                                      in_values=list_[tt][:, c, :], imm_value=LOWEST))
                        both_apart(lambda tt: max_(top[:, tt, c, 8:16], rest[tt][:, 0:NK]))
                        both_apart(lambda tt: max_index(top_i[:, tt, c, 8:16], top[:, tt, c, 8:16], rest[tt][:, 0:NK]))
                    both(lambda tt: copy(top_f[:, tt, :, :], top_i[:, tt, :, :]))
                    both(lambda tt: tt_op(cand[tt][:, :].rearrange("p (i k) -> p i k", i=TOPK),
                                          top[:, tt, 0, :].unsqueeze(2).to_broadcast([P, TOPK, TOPK]),
                                          top[:, tt, 1, :].unsqueeze(1).to_broadcast([P, TOPK, TOPK]), ALU.add))
                    both_apart(lambda tt: max_(best[:, tt, 0:8], cand[tt]))
                    both_apart(lambda tt: max_index(best_i[:, tt, 0:8], best[:, tt, 0:8], cand[tt]))
                    both_apart(lambda tt: replace(out=rest[tt], in_to_replace=best[:, tt, 0:8], in_values=cand[tt],
                                                  imm_value=LOWEST))
                    both_apart(lambda tt: max_(best[:, tt, 8:16], rest[tt]))
                    both_apart(lambda tt: max_index(best_i[:, tt, 8:16], best[:, tt, 8:16], rest[tt]))
                    steps.behind(ts_op(place_i[:, 0, 0, :], best_i[:, 0, :], 4, None, ALU.logical_shift_right))
                    steps.free(ts_op(place_i[:, 1, 0, :], best_i[:, 1, :], 4, None, ALU.logical_shift_right))
                    for tt in range(2):
                        steps.free(ts_op(place_i[:, tt, 1, :], best_i[:, tt, :], TOPK - 1, None, ALU.bitwise_and))
                    steps.free(copy(best_all[:, 0, bass.ds(head, 1), :], best[:, 0, :].unsqueeze(1)))
                    steps.behind(copy(best_all[:, 1, bass.ds(head, 1), :], best[:, 1, :].unsqueeze(1)))
                    both(lambda tt: copy(place_f[:, tt, :, :], place_i[:, tt, :, :]))
                    both(lambda tt: tt_op(onehot[tt], place_f[:, tt, :, :].unsqueeze(3).to_broadcast(sixteens),
                                          iota16[:, :].unsqueeze(1).unsqueeze(1).to_broadcast(sixteens), ALU.is_equal))
                    both(lambda tt: tt_op(onehot[tt], onehot[tt], top_f[:, tt, :, :].unsqueeze(2).to_broadcast(sixteens),
                                          ALU.mult))
                    both(lambda tt: nc.vector.tensor_reduce(best_of[:, tt, :, :], onehot[tt], axis=AX.X, op=ALU.add))
                    here = bass.ds(head * TOPK, TOPK)
                    if h == 0:
                        both(lambda tt: ts_op(pre_idx[:, tt, :], best_of[:, tt, 0, :], float(NK), float(l * NK * NK),
                                              ALU.mult, ALU.add))
                        both(lambda tt: tt_op(pick_idx[:, tt, here], pre_idx[:, tt, :], best_of[:, tt, 1, :], ALU.add))
                    else:
                        both(lambda tt: copy(pick_key[:, tt, :, here], best_of[:, tt, :, :]))

                for first, heads in ((0, EARLY), (EARLY, PH - EARLY)) if h == 0 else ((0, PH),):
                    with steps.loop(heads // 2, 4 * (27 - h)) as i:
                        for n in range(2):
                            dve.wait_ge(scores_ready, i * 2 + (first + n + PK[l, h] + 1 + CREDIT))
                            rank(i * 2 + (first + n))
                    if h == 0 and first == 0:
                        norm(l, 1, 0)
                steps.settle()
                for tt in range(2):
                    j = 2 * half_no(l, h) + tt
                    gates = pick_gate[:, h, tt, :].rearrange("p (h k) -> p h k", h=PH)
                    tt_op(gates, best_all[:, tt, :, :], best_all[:, tt, :, 0:1].to_broadcast([P, PH, TOPK]), ALU.subtract
                          ).then_inc(best_ready, 1)
                    dve.wait_ge(exp_ready, j + 1)
                    steps(nc.vector.tensor_reduce(gate_sum[:, :], gates, axis=AX.X, op=ALU.add))
                    steps(nc.vector.reciprocal(gate_inv[:, :], gate_sum[:, :]))
                    tt_op(gates, gates, gate_inv[:, :].unsqueeze(2).to_broadcast([P, PH, TOPK]), ALU.mult
                          ).then_inc(picks_ready, 1)

            def u_dot(q, b, r):
                dve.wait_ge(u_in[r], (b + q * BATCHES) * 16 + 16)
                stt_op(out=u_rows[:, r, :], in0=u_rows[:, r, :], scalar=1.0, in1=h_rows[:, q % 2, :], op0=ALU.mult, op1=ALU.mult,
                       accum_out=dots[:, bass.ds(b * BATCH + r, 1)]).then_inc(u_used, 1)

            def dots_done(q, b):
                dve.wait_ge(u_used, (b + q * BATCHES) * BATCH + (BATCH + U_CREDIT))
                dve.sem_inc(dots_ready, 1)

            def weigh(q, b):
                dve.wait_ge(gelu_ready, b + (q * BATCHES + 1))
                at = bass.ds(b * BATCH, BATCH)
                tt_op(acts[:, at], acts[:, at], pick_gate[:, 0, q % 2, at], ALU.mult).then_inc(acts_ready, 1)
                dve.wait_ge(acts_ready, b + (q * BATCHES + 1))

            def v_add(q, b, r):
                n = (b + q * BATCHES) * BATCH + r
                dve.wait_ge(v_in[r % VR], (b + q * BATCHES) * (16 * BATCH // VR) + 16 * (r // VR + 1))
                dve.wait_ge(v_used, n + V_CREDIT)
                stt_op(out=y[:, :], in0=v_rows[:, r % VR, :], scalar=acts[:, bass.ds(b * BATCH + r, 1)], in1=y[:, :],
                       op0=ALU.mult, op1=ALU.add).then_inc(v_used, 1)

            def add_peer(source, t, c):
                half = slice(c * 512, (c + 1) * 512)
                steps(tt_op(y_tmp[:, :], source, g2_row[:, half], ALU.mult))
                steps(tt_op(x[:, t, half], x[:, t, half], y_tmp[:, :], ALU.add))

            def peer(l):
                dve.wait_ge(picks_t_ready, l + 1)

                def hots(g, i, s):
                    dve.wait_ge(gates_ready, i * 2 + ((l * ROUNDS + g) * GROUPS + s + 1))
                    for t in range(GROUP):
                        token = i * (2 * GROUP) + (s * GROUP + t)
                        ts_op(hot2[:, s, t, :], iota_keys[:, :], pick_t[:, 1, bass.ds(token, 1)],
                              pick_t[:, 2, bass.ds(token, 1)], ALU.is_equal, ALU.mult)
                    wide = [P, GROUP, ROUND]
                    steps(tt_op(hot1[:, s, :, :], iota_keys[:, g * ROUND:(g + 1) * ROUND].unsqueeze(1).to_broadcast(wide),
                                pick_t[:, 0, bass.ds(i * (2 * GROUP) + s * GROUP, GROUP)].unsqueeze(2).to_broadcast(wide),
                                ALU.is_equal))
                    dve.sem_inc(hots_ready, 1)

                dve.wait_ge(h_rows_ready, 2 * l + 2)
                pairs = GROUPS // 2 // BATCH
                for r in range(BATCH):
                    with steps.loop(pairs, 2) as i:
                        for s in range(2):
                            hots(0, i + r * pairs, s)
                    u_dot(2 * l, 0, r)
                dots_done(2 * l, 0)
                for g in range(ROUNDS):
                    q, first = 2 * l + g // 2, g % 2 * (BATCHES // 2)
                    if g % 2 == 0:
                        steps(nc.vector.memset(y[:, :], 0.0))
                    dve.wait_ge(gates_ready, (l * ROUNDS + g + 1) * GROUPS + CREDIT)

                    def four(b, after):
                        weigh(q, b + first)
                        for n in range(PER_BATCH):
                            dve.wait_ge(e_gelu_ready, b * PER_BATCH + (dense_no(l, g) + n + 1))
                            tt_op(e_act[:, n % 2, :], e_act[:, n % 2, :],
                                  region[:, bass.ds(b * (PER_BATCH * HALF) + (g % 2 * ROUND + n) * HALF, HALF)], ALU.mult
                                  ).then_inc(e_act_ready, 1)
                            if g + 1 < ROUNDS:
                                hots(g + 1, b * (PER_BATCH // 2) + n // 2, n % 2)
                            for r in range(n * BATCH // PER_BATCH, (n + 1) * BATCH // PER_BATCH):
                                if after:
                                    u_dot(*after, r)
                                v_add(q, b + first, r)
                        if after:
                            dots_done(*after)

                    per = PER_BATCH if g + 1 < ROUNDS else 0
                    if g % 2 == 0:
                        with steps.loop(BATCHES // 2, per) as b:
                            four(b, (q, b + 1))
                    else:
                        with steps.loop(BATCHES // 2 - 1, per) as b:
                            four(b, (q, b + (first + 1)))
                        four(BATCHES // 2 - 1, (q + 1, 0) if q % 2 == 0 else None)
                        dve.wait_ge(v_used, (q + 1) * PICKS + V_CREDIT)
                        for c in range(2):
                            add_peer(y[:, c * 512:(c + 1) * 512], q % 2, c)
                dve.sem_inc(x_peer, 2)
                dve.wait_ge(e_out_full, l + 1)
                for tt in range(2):
                    for c in range(2):
                        steps.behind(tt_op(y_tmps[:, c, :], out_e[2 * tt + c][:, :], g2_row[:, c * 512:(c + 1) * 512], ALU.mult))
                    for c in range(2):
                        half = slice(c * 512, (c + 1) * 512)
                        steps.behind(tt_op(x[:, 2 + tt, half], x[:, 2 + tt, half], y_tmps[:, c, :], ALU.add))
                steps.settle()
                dve.sem_inc(x_peer, 2)

            def final():
                dve.wait_ge(final_in, 16)
                for t in range(TILES):
                    if t % 2 == 0:
                        reciprocal_root((N_NORMS + t) // 2)
                    dve.wait_ge(xn_ready, N_NORMS + t + 1)
                    tt_op(x[:, t, :], xn[:, :], final_row, ALU.mult).then_inc(out_ready, 1)

            for what, *at in ORDER:
                if what == "ada" and at[1]:
                    ada(at[0])
                    spread_columns(at[0])
                elif what == "mix":
                    if at[1] == 0:
                        norm(at[0], 0, 0)
                        spread_rows(at[0])
                    conv(at[1]) if at[0] == 0 else attention(at[1])
                elif what == "sel":
                    norm(at[0], at[1], 1)
                    select(*at)
                elif what == "peer":
                    peer(at[0])
                elif what == "final":
                    final()


def kernel(**inputs):
    import numpy as np
    import concourse.bacc as bacc
    from concourse.bass_utils import run_bass_kernel_spmd

    a = {k: np.asarray(v) for k, v in inputs.items()}

    def chunked(w):
        n = w.shape[1]
        return np.ascontiguousarray(w.reshape(KB, P, n // NC, NC).transpose(2, 1, 0, 3)).reshape(n // NC, P, CHUNK)

    def column(v):
        return v.reshape(-1, P).T

    w_in = a["cv_w_in"][0].reshape(D, 2, KB, P).transpose(0, 2, 1, 3).reshape(D, 2 * D)
    arrays = {
        "x": a["x"][0], "w_in": chunked(w_in), "w_out": chunked(a["cv_w_out"][0]),
        "w_qkv": chunked(a["sb_w_qkv"][0]), "w_o": chunked(a["sb_w_o"][0]),
        "b_out": a["cv_b_out"][0], "g_ffn": a["norm_ffn_g"], "final_g": a["final_g"], "ada_b": a["ada_b"],
        "pk_u": a["pk_u"].reshape(DEPTH * NK * NK, D), "pk_v": a["pk_v"].reshape(DEPTH * NK * NK, D),
        "cols": np.concatenate([column(a["c"][0]), column(a["norm_mix_g"].reshape(-1)), column(a["norm_ffn_g"].reshape(-1)),
                                column(a["cv_b_in"][0]),
                                a["cv_w_dw"][0].reshape(WIDTH, KB, P).transpose(2, 1, 0).reshape(P, KB * WIDTH),
                                column(a["cv_b_dw"][0]), column(a["cv_ln_g"][0]), column(a["cv_ln_b"][0])], axis=1),
    }
    arrays["u_t"] = a["pk_u"].reshape(DEPTH * NK, NK, KB, P).transpose(0, 3, 2, 1).reshape(DEPTH * NK, P, D)
    for l in range(DEPTH):
        arrays[f"ada{l}"] = chunked(a["ada_w"][l])
        arrays[f"pk{l}"] = chunked(a["pk_w_q"][l])
        arrays[f"keys{l}"] = a["pk_keys"][l].transpose(3, 0, 1, 2).reshape(P, PH * 2 * NK)

    nc = bacc.Bacc("TRN2", target_bir_lowering=False, num_devices=1)
    feeds, aps = {}, {}
    for name, array in arrays.items():
        array = np.ascontiguousarray(array)
        feeds[f"in_{name}"] = array
        aps[name] = nc.dram_tensor(f"in_{name}", array.shape, mybir.dt.from_np(array.dtype), kind="ExternalInput").ap()
    out = nc.dram_tensor("out", (SEQ, D), F32, kind="ExternalOutput").ap()
    build(nc, aps, out)
    got = run_bass_kernel_spmd(nc, [feeds], core_ids=[0])
    return got.results[0]["out"].reshape(1, SEQ, D)
```
